# Optimizing a Trainium2 kernel written in Bass

```python
import jax, jax.numpy as jnp
from jax import lax
import numpy as np

D_MODEL = 1024
BATCH = 1
SEQ = 4096
DEPTH = 1

POOL_WIDTH = 256
POOL_GROUPS = 4
POOL_WINDOWS = (2, 4, 8, 16)
CONV_WIDTH = 256
CONV_KERNEL = 31
HEAD_DIM = 64
N_Q_HEADS = 8
N_KV_HEADS = 2
Q_PER_KV = N_Q_HEADS // N_KV_HEADS
ATTN_WIDTH = N_Q_HEADS * HEAD_DIM
KV_WIDTH = N_KV_HEADS * HEAD_DIM
WINDOW = 128
BLOCK = 128
D_MIX = POOL_WIDTH + CONV_WIDTH + ATTN_WIDTH
D_IN = 2 * POOL_WIDTH + 3 * CONV_WIDTH + 2 * ATTN_WIDTH + 2 * KV_WIDTH
EPS = 1e-6

kernel_name = "hybrid_pool_conv_swa_block"

def rms_norm(x, g):
    xf = x.astype(jnp.float32)
    y = xf * lax.rsqrt(jnp.mean(xf * xf, axis=-1, keepdims=True) + EPS)
    return (y * g.astype(jnp.float32)).astype(x.dtype)

def layer_norm(x, g, b):
    xf = x.astype(jnp.float32)
    mu = jnp.mean(xf, axis=-1, keepdims=True)
    var = jnp.mean(jnp.square(xf - mu), axis=-1, keepdims=True)
    y = (xf - mu) * lax.rsqrt(var + EPS)
    return (y * g.astype(jnp.float32) + b.astype(jnp.float32)).astype(x.dtype)

def alibi_slopes():
    return jnp.asarray([2.0 ** (-8.0 * (h + 1) / N_Q_HEADS) for h in range(N_Q_HEADS)], dtype=jnp.float32)

def pool_mixer(u, w, scale):
    B, S, _ = u.shape
    gw = POOL_WIDTH // POOL_GROUPS
    uf = u.astype(jnp.float32)
    c = jnp.cumsum(uf, axis=1)
    t = jnp.arange(S, dtype=jnp.float32)[:, None]
    outs = []
    for g, wnd in enumerate(POOL_WINDOWS):
        cg = c[..., g * gw:(g + 1) * gw]
        prev = jnp.pad(cg, ((0, 0), (wnd, 0), (0, 0)))[:, :S]
        cnt = jnp.minimum(t + 1.0, float(wnd))
        outs.append((cg - prev) / cnt)
    pooled = jnp.stack(outs, axis=2)
    diff = (pooled - uf.reshape(B, S, POOL_GROUPS, gw)).astype(u.dtype)
    y = jnp.einsum('bsgc,gcd->bsgd', diff, w).reshape(B, S, POOL_WIDTH)
    return y * scale

def conv_module(a, b, dw, dw_bias, ln_g, ln_b, pw):
    h = a * jax.nn.sigmoid(b)
    h = jnp.pad(h, ((0, 0), (CONV_KERNEL - 1, 0), (0, 0)))
    h = lax.conv_general_dilated(h, dw[:, None, :], window_strides=(1,), padding='VALID',
                                 dimension_numbers=('NWC', 'WIO', 'NWC'),
                                 feature_group_count=CONV_WIDTH) + dw_bias
    h = layer_norm(h, ln_g, ln_b)
    h = jax.nn.silu(h)
    return jnp.einsum('bsc,cd->bsd', h, pw)

def sliding_window_attention(q, k, v, sinks):
    B, S, _ = q.shape
    nb = S // BLOCK
    qb = q.reshape(B, nb, BLOCK, N_KV_HEADS, Q_PER_KV, HEAD_DIM) * (HEAD_DIM ** -0.5)
    kr = jnp.pad(k.reshape(B, nb, BLOCK, N_KV_HEADS, HEAD_DIM), ((0, 0), (1, 0), (0, 0), (0, 0), (0, 0)))
    vr = jnp.pad(v.reshape(B, nb, BLOCK, N_KV_HEADS, HEAD_DIM), ((0, 0), (1, 0), (0, 0), (0, 0), (0, 0)))
    kb = jnp.concatenate([kr[:, :-1], kr[:, 1:]], axis=2)
    vb = jnp.concatenate([vr[:, :-1], vr[:, 1:]], axis=2)
    scores = jnp.einsum('bnqkgd,bnskd->bnkgqs', qb, kb).astype(jnp.float32)
    i = jnp.arange(BLOCK)[:, None]
    j = jnp.arange(2 * BLOCK)[None, :]
    dist = BLOCK + i - j
    in_band = (dist >= 0) & (dist < WINDOW)
    key_exists = ~(((jnp.arange(nb) == 0)[:, None, None]) & (j < BLOCK)[None])
    valid = in_band[None] & key_exists
    bias = -alibi_slopes().reshape(N_KV_HEADS, Q_PER_KV)[:, :, None, None] * dist.astype(jnp.float32)
    scores = jnp.where(valid[None, :, None, None], scores + bias[None, None], -1e30)
    sink = jnp.broadcast_to(sinks.astype(jnp.float32).reshape(N_KV_HEADS, Q_PER_KV)[None, None, :, :, None, None],
                            scores.shape[:-1] + (1,))
    p = jax.nn.softmax(jnp.concatenate([scores, sink], axis=-1), axis=-1)[..., :-1]
    out = jnp.einsum('bnkgqs,bnskd->bnqkgd', p.astype(v.dtype), vb)
    return out.reshape(B, S, ATTN_WIDTH)

def split_columns(proj):
    sizes = (POOL_WIDTH, POOL_WIDTH, CONV_WIDTH, CONV_WIDTH, CONV_WIDTH,
             ATTN_WIDTH, KV_WIDTH, KV_WIDTH, ATTN_WIDTH)
    idx = [int(s) for s in np.cumsum(sizes)[:-1]]
    return jnp.split(proj, idx, axis=-1)

def setup_inputs(seed: int = 0) -> dict:
    key = jax.random.key(seed)
    ks = jax.random.split(key, 14)
    f32 = jnp.float32
    gw = POOL_WIDTH // POOL_GROUPS
    x = jax.random.normal(ks[0], (BATCH, SEQ, D_MODEL), f32)
    ln_g = 1.0 + 0.05 * jax.random.normal(ks[1], (DEPTH, D_MODEL), f32)
    w_in = jax.random.normal(ks[2], (DEPTH, D_MODEL, D_IN), f32) * D_MODEL ** -0.5
    pool_w = jax.random.normal(ks[3], (DEPTH, POOL_GROUPS, gw, gw), f32) * gw ** -0.5
    pool_scale = 0.5 + 0.05 * jax.random.normal(ks[4], (DEPTH, POOL_WIDTH), f32)
    conv_dw = jax.random.normal(ks[5], (DEPTH, CONV_KERNEL, CONV_WIDTH), f32) * CONV_KERNEL ** -0.5
    conv_b = 0.02 * jax.random.normal(ks[6], (DEPTH, CONV_WIDTH), f32)
    conv_ln_g = 1.0 + 0.05 * jax.random.normal(ks[7], (DEPTH, CONV_WIDTH), f32)
    conv_ln_b = 0.02 * jax.random.normal(ks[8], (DEPTH, CONV_WIDTH), f32)
    conv_pw = jax.random.normal(ks[9], (DEPTH, CONV_WIDTH, CONV_WIDTH), f32) * CONV_WIDTH ** -0.5
    attn_sinks = 0.5 * jax.random.normal(ks[10], (DEPTH, N_Q_HEADS), f32)
    w_out = jax.random.normal(ks[11], (DEPTH, D_MIX, D_MODEL), f32) * D_MIX ** -0.5
    final_g = 1.0 + 0.05 * jax.random.normal(ks[12], (D_MODEL,), f32)
    return {"x": x, "ln_g": ln_g, "w_in": w_in, "pool_w": pool_w, "pool_scale": pool_scale,
            "conv_dw": conv_dw, "conv_b": conv_b, "conv_ln_g": conv_ln_g, "conv_ln_b": conv_ln_b,
            "conv_pw": conv_pw, "attn_sinks": attn_sinks, "w_out": w_out, "final_g": final_g}

def reference(x, ln_g, w_in, pool_w, pool_scale, conv_dw, conv_b, conv_ln_g, conv_ln_b,
              conv_pw, attn_sinks, w_out, final_g):
    for l in range(DEPTH):
        h = rms_norm(x, ln_g[l])
        proj = jnp.einsum('bsd,de->bse', h, w_in[l])
        (u_pool, g_pool, c_a, c_b, g_conv, q, k, v, g_attn) = split_columns(proj)
        y_pool = pool_mixer(u_pool, pool_w[l], pool_scale[l])
        y_conv = conv_module(c_a, c_b, conv_dw[l], conv_b[l], conv_ln_g[l], conv_ln_b[l], conv_pw[l])
        y_attn = sliding_window_attention(q, k, v, attn_sinks[l])
        y = jnp.concatenate([y_pool * jax.nn.silu(g_pool),
                             y_conv * jax.nn.silu(g_conv),
                             y_attn * jax.nn.silu(g_attn)], axis=-1)
        x = x + jnp.einsum('bse,ed->bsd', y, w_out[l])
    return rms_norm(x, final_g)


_drawn_inputs = setup_inputs


def setup_inputs(seed=0):
    import zlib

    import numpy as np

    out = dict(_drawn_inputs(seed))
    spreads = {}
    factors = {'ln_g': 2.748,
     'pool_scale': 4.61,
     'conv_b': 8.0,
     'conv_ln_g': 5.353,
     'conv_ln_b': 31.468,
     'attn_sinks': 18.457}
    for name, (base, spread) in spreads.items():
        noise = np.random.default_rng([zlib.crc32(name.encode()), seed]).standard_normal(out[name].shape)
        drawn = base * np.exp(spread * noise) if base else spread * noise
        out[name] = __import__('jax').numpy.asarray(drawn.astype(out[name].dtype))
    for name, factor in factors.items():
        out[name] = (out[name] * factor).astype(out[name].dtype)
    return out
```

```python
from contextlib import ExitStack

import concourse.bass as bass
from concourse import mybir

F32 = mybir.dt.float32
F32R = mybir.dt.float32r
ALU = mybir.AluOpType
ACT = mybir.ActivationFunctionType

P = 128
D = 1024
S = 4096
KT = D // P
TB = 512
NB = S // TB
SUB = TB // P
POOL_W = 256
CONV_W = 256
TAPS = 31
HEADS = 8
KV = 2
GROUP = HEADS // KV
HD = 64
ATTN_W = HEADS * HD
WINDOW = 128
EPS = 1e-6
MASKED = -1e30
CHUNK = 256
POOL_WINDOWS = (2, 4, 8, 16)
HALO = 16
PAD = TAPS - 1

COL_U = 0
COL_GP = COL_U + POOL_W
COL_CA = COL_GP + POOL_W
COL_CB = COL_CA + CONV_W
COL_GC = COL_CB + CONV_W
COL_Q = COL_GC + CONV_W
COL_K = COL_Q + ATTN_W
COL_V = COL_K + KV * HD
COL_GA = COL_V + KV * HD

Y_POOL, Y_CONV, Y_ATTN = 0, 2, 4


def need(engine, sem, count):
    if not isinstance(count, int) or count > 0:
        engine.wait_ge(sem, count)


class Carrier:

    def __init__(self, nc, ctx, name):
        self.nc = nc
        self.cell = ctx.enter_context(nc.sbuf_tensor(name, [P, 2], F32))
        self.ready = ctx.enter_context(nc.semaphore(name + "_ready"))

    def prepare(self, engine):
        engine.memset(self.cell[:], 0.0).then_inc(self.ready, 1)
        engine.wait_ge(self.ready, 1)

    def dve_wait(self, dve, sem, count):
        dve.wait_ge(sem, count)
        if not isinstance(count, int):
            self.nc.vector.tensor_copy(self.cell[:, 0:1], self.cell[:, 1:2])

    def pool_wait(self, pool, sem, count):
        pool.wait_ge(sem, count)
        if not isinstance(count, int):
            self.nc.gpsimd.tensor_tensor(self.cell[:, 0:1], self.cell[:, 1:2], self.cell[:, 1:2], ALU.add)


def identity(nc, pool, ident, sem):
    nc.gpsimd.memset(ident[:], 0.0).then_inc(sem, 1)
    pool.wait_ge(sem, 1)
    nc.gpsimd.affine_select(out=ident[:], in_=ident[:], compare_op=ALU.not_equal, fill=1.0,
                            base=0, pattern=[[-1, P]], channel_multiplier=1).then_inc(sem, 1)


class XStage:

    def __init__(self, nc, ctx, x, ln_g, tag):
        self.nc, self.x, self.ln_g = nc, x, ln_g
        sb = lambda name, shape, dt=F32: ctx.enter_context(nc.sbuf_tensor(tag + name, shape, dt))
        sem = lambda name: ctx.enter_context(nc.semaphore(tag + name))
        self.xs = sb("xs", [P, SUB, D])
        self.squares = sb("squares", [P, D])
        self.sumsq = sb("sumsq", [P, SUB])
        self.meansq = sb("meansq", [P, SUB])
        self.rstd = sb("rstd", [P, SUB])
        self.neg_half = sb("neg_half", [P, SUB])
        self.gain = sb("gain", [P, KT])
        self.ident = sb("ident", [P, P])
        self.hi = sb("xT_hi", [P, KT, TB], F32R)
        self.lo = sb("xT_lo", [P, KT, TB], F32R)
        self.turn = [ctx.enter_context(nc.psum_tensor(f"{tag}turn{b}", [P, TB], F32)) for b in range(2)]
        self.loaded = [sem(f"x_loaded{s}") for s in range(SUB)]
        self.gain_loaded = sem("gain_loaded")
        self.ident_ready = sem("ident_ready")
        self.half_ready = sem("half_ready")
        self.squared = sem("x_squared")
        self.rstd_steps = sem("rstd_steps")
        self.scaled = sem("x_scaled")
        self.turned = sem("x_turned")
        self.hi_done = sem("xT_hi_done")
        self.lo_done = sem("xT_lo_done")

    def load(self, sp, n):
        need(sp, self.turned, KT * n)
        for s in range(SUB):
            sp.dma_start(self.xs[:, s, :], self.x[0, bass.ds(n * TB + s * P, P), :]).then_inc(self.loaded[s], 16)

    def load_gain(self, sp):
        with self.nc.allow_non_contiguous_dma(reason="1024 values, once"):
            sp.dma_start(self.gain[:], self.ln_g[0].rearrange("(k p) -> p k", p=P)).then_inc(self.gain_loaded, 16)

    def square(self, act, n):
        for s in range(SUB):
            act.wait_ge(self.loaded[s], 16 * n + 16)
            if not isinstance(n, int) or n > 0 or s > 0:
                act.wait_ge(self.squared, SUB * n + s)
            self.nc.scalar.activation(self.squares[:], self.xs[:, s, :], ACT.Square,
                                      accum_out=self.sumsq[:, s:s + 1]).then_inc(self.squared, 1)

    def prepare(self, pool, carrier):
        self.carrier = carrier
        self.nc.gpsimd.memset(self.neg_half[:], -0.5).then_inc(self.half_ready, 1)
        identity(self.nc, pool, self.ident, self.ident_ready)
        pool.wait_ge(self.half_ready, 1)

    def scale(self, pool, n):
        nc = self.nc
        self.carrier.pool_wait(pool, self.squared, SUB * n + SUB)
        nc.gpsimd.tensor_scalar(self.meansq[:], self.sumsq[:], 1.0 / D, EPS, ALU.mult, ALU.add).then_inc(self.rstd_steps, 1)
        pool.wait_ge(self.rstd_steps, 2 * n + 1)
        nc.gpsimd.tensor_tensor(self.rstd[:], self.meansq[:], self.neg_half[:], ALU.pow).then_inc(self.rstd_steps, 1)
        self.carrier.pool_wait(pool, self.rstd_steps, 2 * n + 2)
        for s in range(SUB):
            nc.gpsimd.tensor_scalar(self.xs[:, s, :], self.xs[:, s, :], self.rstd[:, s:s + 1], 1.0,
                                    ALU.mult, ALU.mult).then_inc(self.scaled, 1)

    def transpose(self, pe, n, k):
        if k == 0:
            pe.wait_ge(self.scaled, SUB * n + SUB)
            if isinstance(n, int) and n == 0:
                pe.wait_ge(self.ident_ready, 2)
        if k >= 2:
            pe.wait_ge(self.lo_done, KT * n + k - 1)
        for s in range(SUB):
            last = self.nc.tensor.transpose(self.turn[k % 2][:, s * P:(s + 1) * P],
                                            self.xs[:, s, k * P:(k + 1) * P], self.ident[:])
        last.then_inc(self.turned, 1)

    def split_hi(self, act, n, k):
        if isinstance(n, int) and n == 0 and k == 0:
            act.wait_ge(self.gain_loaded, 16)
        act.wait_ge(self.turned, KT * n + k + 1)
        self.nc.scalar.activation(self.hi[:, k, :], self.turn[k % 2][:], ACT.Copy,
                                  scale=self.gain[:, k:k + 1]).then_inc(self.hi_done, 1)

    def split_lo(self, dve, n, k):
        dve.wait_ge(self.hi_done, KT * n + k + 1)
        self.nc.vector.scalar_tensor_tensor(out=self.lo[:, k, :], in0=self.turn[k % 2][:],
                                            scalar=self.gain[:, k:k + 1], in1=self.hi[:, k, :].bitcast(F32),
                                            op0=ALU.mult, op1=ALU.subtract).then_inc(self.lo_done, 1)


def split3(nc, out, w_hi, w_lo, x_hi, x_lo, first, last):
    nc.tensor.matmul(out, w_hi, x_hi, start=first, stop=False)
    nc.tensor.matmul(out, w_lo, x_hi, start=False, stop=False)
    return nc.tensor.matmul(out, w_hi, x_lo, start=False, stop=last)


class Weights:

    def __init__(self, nc, ctx, w_in, cols, stage, tag):
        self.nc, self.w_in, self.cols, self.stage = nc, w_in, cols, stage
        n = len(cols)
        self.hi = ctx.enter_context(nc.sbuf_tensor(tag + "w_hi", [P, n, KT, CHUNK], F32R))
        self.lo = ctx.enter_context(nc.sbuf_tensor(tag + "w_lo", [P, n, KT, CHUNK], F32R))
        sem = lambda name: ctx.enter_context(nc.semaphore(tag + name))
        self.loaded = [sem("w_loaded0"), sem("w_loaded1")]
        self.hi_done = sem("w_hi_done")
        self.lo_done = sem("w_lo_done")

    def load(self, sp, c):
        need(sp, self.lo_done, c - 1)
        col = self.cols[c]
        firsts = [col, col + P] if isinstance(col, int) else [col[0] + col[1] * P, col[0] + GROUP * HD + col[1] * P]
        for half, first in enumerate(firsts):
            sp.dma_start(self.stage[c % 2][:, :, half * P:(half + 1) * P],
                         self.w_in[0, :, first:first + P].rearrange("(k p) c -> p k c", p=P)).then_inc(self.loaded[c % 2], 16)

    def parts(self, c, whole):
        staged = self.stage[c % 2]
        if isinstance(self.cols[c], int):
            return [(staged, whole[:, c])]
        heads = lambda t: staged.rearrange("p k (s t d) -> p k s t d", s=KV, t=2)[:, :, :, t, :]
        tile = lambda t: whole[:, c, :, t * P:(t + 1) * P].rearrange("p k (s d) -> p k s d", s=KV)
        return [(heads(t), tile(t)) for t in range(2)]

    def split_hi(self, act, c):
        act.wait_ge(self.loaded[c % 2], 32 * (c // 2) + 32)
        for staged, hi in self.parts(c, self.hi):
            last = self.nc.scalar.activation(hi, staged, ACT.Copy)
        last.then_inc(self.hi_done, 1)

    def split_lo(self, dve, c):
        dve.wait_ge(self.hi_done, c + 1)
        for (staged, lo), (_, hi) in zip(self.parts(c, self.lo), self.parts(c, self.hi)):
            last = self.nc.vector.tensor_tensor(lo, staged, hi.bitcast(F32), ALU.subtract)
        last.then_inc(self.lo_done, 1)


def attention_phase(nc, x, ln_g, w_in, attn_sinks, y_scratch):
    ctx = ExitStack()
    with ctx:
        sb = lambda name, shape, dt=F32: ctx.enter_context(nc.sbuf_tensor("a_" + name, shape, dt))
        sem = lambda name: ctx.enter_context(nc.semaphore("a_" + name))
        pool_carrier = Carrier(nc, ctx, "a_pool_carrier")
        dve_carrier = Carrier(nc, ctx, "a_dve_carrier")
        st = XStage(nc, ctx, x, ln_g, "a_")
        probs = sb("probs", [P, 2, HEADS, 2 * P])
        stage = [probs[:, b].rearrange("p h j -> p (h j)").rearrange("p (k c) -> p k c", k=KT) for b in range(2)]
        w = Weights(nc, ctx, w_in, [COL_K, (COL_Q, 0), (COL_Q, 1), (COL_GA, 0), (COL_GA, 1)], stage, "a_")

        q = sb("q", [P, GROUP, TB])
        k = sb("k", [P, P + TB])
        vT = sb("vT", [P, TB])
        v = sb("v", [P, 1 + SUB, P])
        gate = sb("gate", [P, GROUP, TB])
        tanh = sb("tanh", [P, 2, TB])
        pT = sb("pT", [P, 2, KV, GROUP * P])
        y = sb("y", [P, GROUP, TB])
        bias = sb("bias", [P, HEADS, 2 * P])
        dist = sb("dist", [P, 2 * P])
        sinks = sb("sinks", [P, HEADS])
        rowmax = sb("rowmax", [P, 2, HEADS])
        negmax = sb("negmax", [P, 2, HEADS])
        sinkdiff = sb("sinkdiff", [P, 2, HEADS])
        sinkexp = sb("sinkexp", [P, 2, HEADS])
        rowsum = sb("rowsum", [P, 2, HEADS])
        denom = sb("denom", [P, 2, HEADS])
        inv = sb("inv", [P, 2, HEADS])
        neg_one = sb("neg_one", [P, HEADS])

        proj = [ctx.enter_context(nc.psum_tensor(f"a_proj{b}", [P, TB], F32)) for b in range(2)]
        score = [ctx.enter_context(nc.psum_tensor(f"a_score{b}", [P, 2, 2 * P], F32)) for b in range(4)]

        consts = sem("consts")
        halo_zero = sem("halo_zero")
        sinks_loaded = sem("sinks_loaded")
        bias_ready = sem("bias_ready")
        bias_step = sem("bias_step")
        proj_full = sem("proj_full")
        proj_free = [sem("proj_free0"), sem("proj_free1")]
        k_halo = sem("k_halo")
        v_halo = sem("v_halo")
        v_turned = sem("v_turned")
        v_ready = sem("v_ready")
        score_full = sem("score_full")
        score_taken = sem("score_taken")
        row_step = sem("row_step")
        max_ready = sem("max_ready")
        sink_done = sem("sink_done")
        exp_done = sem("exp_done")
        den_step = sem("den_step")
        probs_ready = sem("probs_ready")
        p_turned = sem("p_turned")
        pT_act = sem("pT_act")
        pT_dve = sem("pT_dve")
        tanh_done = sem("tanh_done")
        gated = sem("gated")
        y_stored = sem("y_stored")

        SLOT = {name: p for p, name in enumerate(
            ["k", "v", "o3", "q0", "q1", "q2", "q3", "g0", "g1", "o0", "g2", "o1", "g3", "o2"])}
        USES = len(SLOT)

        def early(n, p):
            return isinstance(n, int) and n == 0 and p < SLOT["o3"]

        def filled(n, p):
            return USES * n + p + (1 if early(n, p) else 0)

        def earlier(n, p):
            return USES // 2 * n + p // 2 - (0 if p % 2 or early(n, p) else 1)

        def slot(name):
            return SLOT[name]

        block = ctx.enter_context(nc.Block())

        @block.sync
        def _(sp):
            st.load(sp, 0)
            w.load(sp, 0)
            st.load_gain(sp)
            sp.dma_start(sinks[:], attn_sinks[0:1, :].to_broadcast([P, HEADS])).then_inc(sinks_loaded, 16)
            for c in range(1, 5):
                w.load(sp, c)

            def store(n):
                sp.wait_ge(gated, n + 1)
                sp.dma_start(y_scratch[Y_ATTN:Y_ATTN + GROUP, :, bass.ds(n * TB, TB)].rearrange("t p c -> p t c"),
                             y[:]).then_inc(y_stored, 16)

            st.load(sp, 1)
            with sp.Fori(1, NB - 1) as n:
                store(n - 1)
                st.load(sp, n + 1)
            store(NB - 2)
            store(NB - 1)
            sp.wait_ge(y_stored, 16 * NB)

        @block.gpsimd
        def _(pool):
            carrier = pool_carrier
            carrier.prepare(pool)
            nc.gpsimd.iota(dist[:], pattern=[[-1, 2 * P]], base=P, channel_multiplier=1,
                           allow_small_or_imprecise_dtypes=True).then_inc(bias_step, 1)
            nc.gpsimd.memset(neg_one[:], -1.0).then_inc(consts, 1)
            st.prepare(pool, carrier)
            st.scale(pool, 0)
            pool.wait_ge(bias_step, 1)
            pool.wait_ge(consts, 1)

            def alibi(lo, hi, steps):
                for h in range(HEADS):
                    last = nc.gpsimd.tensor_scalar(bias[:, h, lo:hi], dist[:, lo:hi], -(2.0 ** (-8.0 * (h + 1) / HEADS)),
                                                   1.0, ALU.mult, ALU.mult)
                last.then_inc(bias_step, 1)
                pool.wait_ge(bias_step, steps + 1)
                part = bias[:, :, lo:hi]
                nc.gpsimd.affine_select(out=part, in_=part, compare_op=ALU.is_ge, fill=MASKED, base=P - lo,
                                        pattern=[[0, HEADS], [-1, hi - lo]], channel_multiplier=1).then_inc(bias_step, 1)
                pool.wait_ge(bias_step, steps + 2)
                nc.gpsimd.affine_select(out=part, in_=part, compare_op=ALU.is_ge, fill=MASKED, base=WINDOW - 1 - P + lo,
                                        pattern=[[0, HEADS], [1, hi - lo]], channel_multiplier=-1).then_inc(bias_ready, 1)

            nc.gpsimd.memset(bias[:, :, 0:P], MASKED).then_inc(consts, 1)
            pool.wait_ge(consts, 2)
            alibi(P, 2 * P, 1)

            def normalise(n, j):
                m, b = 4 * n + j, j % 2
                for kv in range(KV):
                    heads = slice(kv * GROUP, (kv + 1) * GROUP)
                    pool.wait_ge(exp_done, 2 * m + kv + 1)
                    nc.gpsimd.tensor_tensor(denom[:, b, heads], rowsum[:, b, heads], sinkexp[:, b, heads],
                                            ALU.add).then_inc(den_step, 1)
                    pool.wait_ge(den_step, 4 * m + 2 * kv + 1)
                    nc.gpsimd.tensor_tensor(inv[:, b, heads], denom[:, b, heads], neg_one[:, heads],
                                            ALU.pow).then_inc(den_step, 1)
                    carrier.pool_wait(pool, den_step, 4 * m + 2 * kv + 2)
                    for t in range(GROUP):
                        h = kv * GROUP + t
                        last = nc.gpsimd.tensor_scalar(probs[:, b, h, :], probs[:, b, h, :], inv[:, b, h:h + 1], 0.5,
                                                       ALU.mult, ALU.mult)
                    last.then_inc(probs_ready, 1)

            def gate_output(n, at):
                pool.wait_ge(proj_free[at[1] % 2], earlier(*at) + 1)
                for t in range(GROUP):
                    last = nc.gpsimd.tensor_tensor(y[:, t, :], y[:, t, :], gate[:, t, :], ALU.mult)
                last.then_inc(gated, 1)

            def body(n, more):
                if not isinstance(n, int) or n > 0:
                    gate_output(n - 1, (n, slot("o3")))
                if more:
                    st.scale(pool, n + 1)
                if isinstance(n, int) and n == 0:
                    pool.wait_ge(score_taken, 2)
                    alibi(0, P, 3)
                for j in range(SUB):
                    normalise(n, j)

            body(0, True)
            with pool.Fori(1, NB - 1) as n:
                body(n, True)
            body(NB - 1, False)
            gate_output(NB - 1, (NB, 0))

        @block.scalar
        def _(act):
            st.square(act, 0)
            for c in range(5):
                w.split_hi(act, c)

            def copy_out(n, p, out, scale=1.0):
                act.wait_ge(proj_full, filled(n, p))
                nc.scalar.activation(out, proj[p % 2][:], ACT.Copy, scale=scale).then_inc(proj_free[p % 2], 1)

            def exps(n, j, kv):
                m, b = 4 * n + j, j % 2
                heads = slice(kv * GROUP, (kv + 1) * GROUP)
                act.wait_ge(max_ready, 2 * m + kv + 1)
                nc.scalar.activation(sinkexp[:, b, heads], sinkdiff[:, b, heads], ACT.Exp)
                for t in range(GROUP):
                    h = kv * GROUP + t
                    last = nc.scalar.activation(probs[:, b, h, :], probs[:, b, h, :], ACT.Exp,
                                                bias=negmax[:, b, h:h + 1], accum_out=rowsum[:, b, h:h + 1])
                last.then_inc(exp_done, 1)

            def pT_copy(m, kv):
                act.wait_ge(p_turned, 4 * m + 2 * kv + 1)
                nc.scalar.activation(pT[:, 0, kv, :], st.turn[0][:], ACT.Copy).then_inc(pT_act, 1)

            def gate_tanh(n, t):
                p = slot(f"g{t}")
                act.wait_ge(proj_full, filled(n, p))
                nc.scalar.activation(tanh[:, t % 2, :], proj[p % 2][:], ACT.Tanh, scale=0.5).then_inc(tanh_done, 1)

            def body(n, more):
                first = isinstance(n, int) and n == 0
                for kk in range(KT):
                    st.split_hi(act, n, kk)
                act.wait_ge(proj_full, filled(n, slot("k")))
                if first:
                    act.wait_ge(halo_zero, 2)
                else:
                    nc.scalar.activation(k[:, 0:P], k[:, TB:TB + P], ACT.Copy).then_inc(k_halo, 1)
                    act.wait_ge(k_halo, n)
                copy_out(n, slot("k"), k[:, P:])
                if not first:
                    pT_copy(4 * n - 1, 0)
                    pT_copy(4 * n - 1, 1)
                copy_out(n, slot("v"), vT[:])
                copy_out(n, slot("q0"), q[:, 0, :], HD ** -0.5)
                act.wait_ge(v_turned, n + 1)
                if not first:
                    nc.scalar.activation(v[:, 0, :], v[:, SUB, :], ACT.Copy).then_inc(v_halo, 1)
                    act.wait_ge(v_halo, n)
                nc.scalar.activation(v[:, 1:, :].rearrange("p a d -> p (a d)"), score[0][:].rearrange("p a b -> p (a b)"),
                                     ACT.Copy).then_inc(v_ready, 1)
                for t in range(1, GROUP):
                    copy_out(n, slot(f"q{t}"), q[:, t, :], HD ** -0.5)
                if more:
                    st.square(act, n + 1)
                for j in range(SUB):
                    exps(n, j, 0)
                    if j:
                        pT_copy(4 * n + j - 1, 0)
                    exps(n, j, 1)
                    if j:
                        pT_copy(4 * n + j - 1, 1)
                    gate_tanh(n, j)

            body(0, True)
            with act.Fori(1, NB - 1) as n:
                body(n, True)
            body(NB - 1, False)
            pT_copy(4 * NB - 1, 0)
            pT_copy(4 * NB - 1, 1)

        @block.vector
        def _(dve):
            carrier = dve_carrier
            carrier.prepare(dve)
            nc.vector.memset(k[:, 0:P], 0.0).then_inc(halo_zero, 1)
            nc.vector.memset(v[:, 0, :], 0.0).then_inc(halo_zero, 1)
            for c in range(5):
                w.split_lo(dve, c)
            dve.wait_ge(sinks_loaded, 16)

            def take_scores(n, j):
                m, b = 4 * n + j, j % 2
                if isinstance(n, int) and n == 0:
                    dve.wait_ge(bias_ready, 1 if j == 0 else 2)
                for kv in range(KV):
                    heads = slice(kv * GROUP, (kv + 1) * GROUP)
                    carrier.dve_wait(dve, score_full, 2 * m + kv + 1)
                    for t in range(GROUP):
                        h = kv * GROUP + t
                        last = nc.vector.tensor_tensor_reduce(
                            out=probs[:, b, h, :], in0=score[h // 2][:, h % 2, :], in1=bias[:, h, :], scale=1.0,
                            scalar=sinks[:, h:h + 1], op0=ALU.add, op1=ALU.max, accum_out=rowmax[:, b, h:h + 1])
                    last.then_inc(score_taken, 1)
                    dve.wait_ge(score_taken, 2 * m + kv + 1)
                    nc.vector.tensor_scalar(negmax[:, b, heads], rowmax[:, b, heads], -1.0, None, ALU.mult).then_inc(row_step, 1)
                    nc.vector.tensor_tensor(sinkdiff[:, b, heads], sinks[:, heads], rowmax[:, b, heads],
                                            ALU.subtract).then_inc(max_ready, 1)

            def pT_copy(m, kv):
                dve.wait_ge(p_turned, 4 * m + 2 * kv + 2)
                nc.vector.tensor_copy(pT[:, 1, kv, :], st.turn[1][:]).then_inc(pT_dve, 1)

            def gate_make(n, t):
                p = slot(f"g{t}")
                if t == 0:
                    need(dve, gated, n)
                dve.wait_ge(tanh_done, GROUP * n + t + 1)
                nc.vector.scalar_tensor_tensor(out=gate[:, t, :], in0=tanh[:, t % 2, :], scalar=1.0, in1=proj[p % 2][:],
                                               op0=ALU.add, op1=ALU.mult).then_inc(proj_free[p % 2], 1)

            def output(n, j, at):
                dve.wait_ge(proj_full, filled(*at))
                if j == 0:
                    need(dve, y_stored, 16 * n)
                nc.vector.tensor_copy(y[:, :, j * P:(j + 1) * P],
                                      proj[at[1] % 2][:].rearrange("p (t c) -> p t c", t=GROUP)).then_inc(proj_free[at[1] % 2], 1)

            def body(n):
                first = isinstance(n, int) and n == 0
                for kk in range(KT):
                    st.split_lo(dve, n, kk)
                if not first:
                    pT_copy(4 * n - 1, 0)
                    pT_copy(4 * n - 1, 1)
                    output(n - 1, 3, (n, slot("o3")))
                for j in range(SUB):
                    take_scores(n, j)
                    if j:
                        pT_copy(4 * n + j - 1, 0)
                        pT_copy(4 * n + j - 1, 1)
                    gate_make(n, j)
                    if j:
                        output(n, j - 1, (n, slot(f"o{j - 1}")))

            body(0)
            with dve.Fori(1, NB) as n:
                body(n)
            pT_copy(4 * NB - 1, 0)
            pT_copy(4 * NB - 1, 1)
            output(NB - 1, 3, (NB, 0))

        @block.tensor
        def _(pe):
            def weight(name):
                c, half = (0, "kv".index(name)) if name in "kv" else (1 + 2 * (name[0] == "g") + int(name[1]) // 2, int(name[1]) % 2)
                return lambda part, kk: part[:, c, kk, half * P:(half + 1) * P]

            def project(n, name, between=None):
                p = slot(name)
                wt = weight(name)
                need(pe, proj_free[p % 2], earlier(n, p))
                if isinstance(n, int) and n == 0:
                    pe.wait_ge(w.lo_done, {"k": 1, "v": 1, "q": 3, "g": 5}[name[0]])
                for kk in range(KT):
                    if name == "k":
                        pe.wait_ge(st.lo_done, KT * n + kk + 1)
                    last = split3(nc, proj[p % 2][:], wt(w.hi, kk), wt(w.lo, kk), st.hi[:, kk, :], st.lo[:, kk, :],
                                  kk == 0, kk == KT - 1)
                    if between and kk < KT - 1:
                        between(kk)
                last.then_inc(proj_full, 1)

            def scores(n, j):
                m = 4 * n + j
                for kv in range(KV):
                    rows = slice(kv * HD, (kv + 1) * HD)
                    need(pe, score_taken, 2 * (m - 1) + kv + 1)
                    for t in range(GROUP):
                        h = kv * GROUP + t
                        last = nc.tensor.matmul(score[h // 2][:, h % 2, :], q[rows, t, j * P:(j + 1) * P],
                                                k[rows, j * P:(j + 2) * P], start=True, stop=True)
                    last.then_inc(score_full, 1)

            def turn_probs(m, j, kv):
                for kt in range(2):
                    pe.wait_ge(probs_ready, 2 * m + kv + 1)
                    if kv == 1:
                        pe.wait_ge(pT_dve if kt else pT_act, 2 * m + 1)
                    for t in range(GROUP):
                        last = nc.tensor.transpose(st.turn[kt][:, t * P:(t + 1) * P],
                                                   probs[:, j % 2, kv * GROUP + t, kt * P:(kt + 1) * P], st.ident[:])
                    last.then_inc(p_turned, 1)

            def attend(m, j, at):
                p = at[1]
                need(pe, proj_free[p % 2], earlier(*at))
                pe.wait_ge(pT_act, 2 * m + 2)
                pe.wait_ge(pT_dve, 2 * m + 2)
                for kt in range(2):
                    for kv in range(KV):
                        rows = slice(kv * HD, (kv + 1) * HD)
                        last = nc.tensor.matmul(proj[p % 2][rows, :], v[:, j + kt, rows], pT[:, kt, kv, :],
                                                start=(kt == 0), stop=(kt == 1))
                last.then_inc(proj_full, 1)

            def body(n):
                first = isinstance(n, int) and n == 0
                st.transpose(pe, n, 0)
                st.transpose(pe, n, 1)
                project(n, "k", lambda kk: st.transpose(pe, n, kk + 2) if kk + 2 < KT else None)
                if first:
                    project(n, "v")
                else:
                    project(n, "v", lambda kk: turn_probs(4 * n - 1, 3, kk // 3 - 1) if kk in (3, 6) else None)
                    attend(4 * n - 1, 3, (n, slot("o3")))
                project(n, "q0")
                need(pe, score_taken, 8 * n)
                pe.wait_ge(proj_free[1], earlier(n, slot("v")) + 1)
                for s in range(SUB):
                    last = nc.tensor.transpose(score[0][:].rearrange("p a b -> p (a b)")[:, s * P:(s + 1) * P],
                                               vT[:, s * P:(s + 1) * P], st.ident[:])
                last.then_inc(v_turned, 1)
                for t in range(1, GROUP):
                    project(n, f"q{t}")
                pe.wait_ge(v_ready, n + 1)
                for name in ("q2", "q3"):
                    pe.wait_ge(proj_free[slot(name) % 2], earlier(n, slot(name)) + 1)
                for j in range(SUB):
                    scores(n, j)
                    if j == 0:
                        project(n, "g0")
                    else:
                        m = 4 * n + j - 1
                        project(n, f"g{j}", lambda kk: turn_probs(m, j - 1, kk // 3 - 1) if kk in (3, 6) else None)
                        attend(m, j - 1, (n, slot(f"o{j - 1}")))

            body(0)
            with pe.Fori(1, NB) as n:
                body(n)
            for kv in range(KV):
                turn_probs(4 * NB - 1, 3, kv)
            attend(4 * NB - 1, 3, (NB, 0))


def mixer_phase(nc, x, ln_g, w_in, pool_w, pool_scale, conv_dw, conv_b, conv_ln_g, conv_ln_b, conv_pw, y_scratch):
    ctx = ExitStack()
    with ctx:
        sb = lambda name, shape, dt=F32: ctx.enter_context(nc.sbuf_tensor("m_" + name, shape, dt))
        sem = lambda name: ctx.enter_context(nc.semaphore("m_" + name))
        pool_carrier = Carrier(nc, ctx, "m_pool_carrier")
        dve_carrier = Carrier(nc, ctx, "m_dve_carrier")
        st = XStage(nc, ctx, x, ln_g, "m_")
        stage_buf = sb("stage", [P, 2, KT, CHUNK])
        w = Weights(nc, ctx, w_in, [COL_CB, COL_CA, COL_U, COL_GP, COL_GC], [stage_buf[:, 0], stage_buf[:, 1]], "m_")
        CHUNK_OF = {"cb": 0, "ca": 1, "u": 2, "gp": 3, "gc": 4}

        sig = sb("sig", [P, 2, TB])
        h = sb("h", [P, 2, PAD + TB])
        conv = sb("conv", [P, 2, TB])
        taps = sb("taps", [P, 2, TAPS])
        conv_bias = sb("conv_bias", [P, 2])
        ln_gain = sb("ln_gain", [P, 2])
        ln_bias = sb("ln_bias", [P, 2])
        stats = sb("stats", [P, SUB, 6])
        meanvar = sb("meanvar", [P, SUB, 2])
        var_eps = sb("var_eps", [P, SUB])
        ln_rstd = sb("ln_rstd", [P, SUB])
        z = sb("z", [P, SUB, CONV_W])
        hs = sb("hs", [P, 2, TB])
        pw = sb("pw", [P, 2, CONV_W])
        u = sb("u", [P, 2, HALO + TB])
        sums = sb("sums", [P, 2, 2, HALO + TB])
        diff = sb("diff", [P, 2, TB])
        count = sb("count", [P, 2, HALO])
        widen = sb("widen", [P, 2, HALO])
        pool_lhs = sb("pool_lhs", [P, 2, P])
        pscale = sb("pscale", [P, 2])
        gate_p = sb("gate_p", [P, 2, TB])
        gate_c = sb("gate_c", [P, 2, TB])
        y_pool = sb("y_pool", [P, 2, TB])
        y_conv = sb("y_conv", [P, 2, TB])

        proj = [ctx.enter_context(nc.psum_tensor(f"m_proj{b}", [P, TB], F32)) for b in range(2)]
        tok = [ctx.enter_context(nc.psum_tensor(f"m_tok{b}", [P, 2, CONV_W], F32)) for b in range(2)]
        feat = [ctx.enter_context(nc.psum_tensor(f"m_feat{b}", [P, TB], F32)) for b in range(2)]

        small_loaded = sem("small_loaded")
        pool_w_zero = sem("pool_w_zero")
        halo_zero = sem("halo_zero")
        taps_ready = sem("taps_ready")
        count_step = sem("count_step")
        widen_ready = sem("widen_ready")
        sums_done = sem("sums_done")
        means_done = sem("means_done")
        proj_full = sem("proj_full")
        proj_free = [sem("proj_free0"), sem("proj_free1")]
        h_halo = sem("h_halo")
        h_ready = sem("h_ready")
        tap_done = [sem("tap_done0"), sem("tap_done1")]
        conv_turned = sem("conv_turned")
        stats_done = sem("stats_done")
        meanvar_done = sem("meanvar_done")
        rstd_step = sem("rstd_step")
        z_done = sem("z_done")
        z_turned = sem("z_turned")
        hs_done = sem("hs_done")
        u_halo = sem("u_halo")
        pool_step = sem("pool_step")
        diff_done = sem("diff_done")
        y_pool_stored = sem("y_pool_stored")
        y_conv_stored = sem("y_conv_stored")

        SLOT = {name: p for p, name in enumerate(
            ["cb0", "cb1", "ca0", "ca1", "u0", "u1", "pw0", "pw1", "gp0", "gp1", "gc0", "gc1", "po0", "po1"])}
        USES = len(SLOT)

        def early(n, p):
            return isinstance(n, int) and n == 0 and p < SLOT["pw0"]

        def filled(n, p):
            return USES * n + p + 1 - (0 if early(n, p) else 2)

        def earlier(n, p):
            return USES // 2 * n + p // 2 - (0 if early(n, p) else 1)

        block = ctx.enter_context(nc.Block())

        @block.sync
        def _(sp):
            st.load(sp, 0)
            w.load(sp, 0)
            st.load_gain(sp)
            w.load(sp, 1)
            with nc.allow_non_contiguous_dma(reason="per-channel constants, once"):
                for i in range(2):
                    cols = slice(i * P, (i + 1) * P)
                    sp.dma_start(taps[:, i, :], conv_dw[0, :, cols].rearrange("j p -> p j")).then_inc(small_loaded, 16)
                    for dst, src in ((conv_bias, conv_b), (ln_gain, conv_ln_g), (ln_bias, conv_ln_b), (pscale, pool_scale)):
                        sp.dma_start(dst[:, i:i + 1], src[0, cols].rearrange("(p a) -> p a", a=1)).then_inc(small_loaded, 16)
            sp.dma_start(pw[:], conv_pw[0].rearrange("(i p) d -> p i d", p=P)).then_inc(small_loaded, 16)
            sp.wait_ge(pool_w_zero, 1)
            for g in range(4):
                half = slice(g % 2 * 64, g % 2 * 64 + 64)
                sp.dma_start(pool_lhs[half, g // 2, half], pool_w[0, g]).then_inc(small_loaded, 16)
            for c in range(2, 5):
                w.load(sp, c)

            def store_pool(n):
                sp.wait_ge(proj_free[0], earlier(n, SLOT["po0"]) + 1)
                sp.wait_ge(proj_free[1], earlier(n, SLOT["po1"]) + 1)
                sp.dma_start(y_scratch[Y_POOL:Y_POOL + 2, :, bass.ds(n * TB, TB)].rearrange("t p c -> p t c"),
                             y_pool[:]).then_inc(y_pool_stored, 16)

            def store_conv(n, at):
                sp.wait_ge(proj_free[0], earlier(at[0], at[1]) + 1)
                sp.wait_ge(proj_free[1], earlier(at[0], at[1] + 1) + 1)
                sp.dma_start(y_scratch[Y_CONV:Y_CONV + 2, :, bass.ds(n * TB, TB)].rearrange("t p c -> p t c"),
                             y_conv[:]).then_inc(y_conv_stored, 16)

            st.load(sp, 1)
            store_pool(0)
            with sp.Fori(1, NB - 1) as n:
                st.load(sp, n + 1)
                store_conv(n - 1, (n, SLOT["pw0"]))
                store_pool(n)
            store_conv(NB - 2, (NB - 1, SLOT["pw0"]))
            store_pool(NB - 1)
            store_conv(NB - 1, (NB, 0))
            sp.wait_ge(y_pool_stored, 16 * NB)
            sp.wait_ge(y_conv_stored, 16 * NB)

        SMALL = 16 * (2 * 5 + 1 + 4)

        @block.gpsimd
        def _(pool):
            carrier = pool_carrier
            carrier.prepare(pool)
            nc.gpsimd.memset(pool_lhs[:], 0.0).then_inc(pool_w_zero, 1)
            for i in range(2):
                nc.gpsimd.iota(count[:, i, :], pattern=[[1, HALO]], base=1, channel_multiplier=0,
                               allow_small_or_imprecise_dtypes=True).then_inc(count_step, 1)
            st.prepare(pool, carrier)
            st.scale(pool, 0)

            def window_sums(n):
                pool.wait_ge(proj_free[0], earlier(n, SLOT["u0"]) + 1)
                pool.wait_ge(proj_free[1], earlier(n, SLOT["u1"]) + 1)
                step = 4 * n
                for i in range(2):
                    cur, width = u[:, i, :], 1
                    for level in range(2 * (i + 1)):
                        dst = sums[:, i, level % 2, :]
                        add = nc.gpsimd.tensor_tensor(dst[:, 2 * width:], cur[:, 2 * width:], cur[:, width:HALO + TB - width],
                                                      ALU.add)
                        cur, width = dst, 2 * width
                        if level < 2 * i + 1:
                            add.then_inc(pool_step, 1)
                            step += 1
                            pool.wait_ge(pool_step, step)
                    add.then_inc(sums_done, 1)

            def window_diffs(n):
                for i in range(2):
                    pool.wait_ge(means_done, 2 * n + i + 1)
                    if isinstance(n, int) and n == 0:
                        nc.gpsimd.tensor_tensor(diff[:, i, 0:HALO], diff[:, i, 0:HALO], widen[:, i, :],
                                                ALU.mult).then_inc(widen_ready, 1)
                        pool.wait_ge(widen_ready, 2 + i)
                    nc.gpsimd.tensor_tensor(diff[:, i, :], diff[:, i, :], u[:, i, HALO:], ALU.subtract).then_inc(diff_done, 1)

            def layer_norm_rstd(n):
                carrier.pool_wait(pool, meanvar_done, SUB * n + SUB)
                nc.gpsimd.tensor_scalar(var_eps[:], meanvar[:, :, 1], EPS, 1.0, ALU.add, ALU.mult).then_inc(rstd_step, 1)
                pool.wait_ge(rstd_step, 2 * n + 1)
                nc.gpsimd.tensor_tensor(ln_rstd[:], var_eps[:], st.neg_half[:], ALU.pow).then_inc(rstd_step, 1)

            def body(n, more):
                if isinstance(n, int) and n == 0:
                    pool.wait_ge(widen_ready, 1)
                else:
                    layer_norm_rstd(n - 1)
                window_sums(n)
                window_diffs(n)
                if more:
                    st.scale(pool, n + 1)

            body(0, True)
            with pool.Fori(1, NB - 1) as n:
                body(n, True)
            body(NB - 1, False)
            layer_norm_rstd(NB - 1)

        @block.scalar
        def _(act):
            st.square(act, 0)
            for c in range(5):
                w.split_hi(act, c)
            act.wait_ge(small_loaded, SMALL)

            def from_proj(n, name, out, func, scale=1.0):
                p = SLOT[name]
                act.wait_ge(proj_full, filled(n, p))
                nc.scalar.activation(out, proj[p % 2][:], func, scale=scale).then_inc(proj_free[p % 2], 1)

            def norm_silu(n):
                for i in range(2):
                    act.wait_ge(z_turned, 2 * n + i + 1)
                    nc.scalar.activation(hs[:, i, :], feat[i][:], ACT.Silu, scale=ln_gain[:, i:i + 1],
                                         bias=ln_bias[:, i:i + 1]).then_inc(hs_done, 1)

            def window_means(n):
                for i in range(2):
                    act.wait_ge(sums_done, 2 * n + i + 1)
                    for g in (2 * i, 2 * i + 1):
                        half = slice(g % 2 * 64, g % 2 * 64 + 64)
                        last = nc.scalar.activation(diff[half, i, :], sums[half, i, g % 2, HALO:], ACT.Copy,
                                                    scale=1.0 / POOL_WINDOWS[g])
                    last.then_inc(means_done, 1)

            def body(n, more):
                first = isinstance(n, int) and n == 0
                for kk in range(KT):
                    st.split_hi(act, n, kk)
                for i in range(2):
                    from_proj(n, f"cb{i}", sig[:, i, :], ACT.Tanh, 0.5)
                act.wait_ge(proj_full, filled(n, SLOT["u0"]))
                if first:
                    act.wait_ge(halo_zero, 2)
                else:
                    act.wait_ge(diff_done, 2 * n)
                    nc.scalar.activation(u[:, :, 0:HALO], u[:, :, TB:], ACT.Copy).then_inc(u_halo, 1)
                    act.wait_ge(u_halo, n)
                for i in range(2):
                    from_proj(n, f"u{i}", u[:, i, HALO:], ACT.Copy)
                if not first:
                    norm_silu(n - 1)
                for i in range(2):
                    from_proj(n, f"gp{i}", gate_p[:, i, :], ACT.Silu)
                window_means(n)
                for i in range(2):
                    from_proj(n, f"gc{i}", gate_c[:, i, :], ACT.Silu)
                if more:
                    st.square(act, n + 1)

            body(0, True)
            with act.Fori(1, NB - 1) as n:
                body(n, True)
            body(NB - 1, False)
            norm_silu(NB - 1)

        @block.vector
        def _(dve):
            carrier = dve_carrier
            carrier.prepare(dve)
            nc.vector.memset(h[:, :, 0:PAD], 0.0).then_inc(halo_zero, 1)
            nc.vector.memset(u[:, :, 0:HALO], 0.0).then_inc(halo_zero, 1)
            for c in range(5):
                w.split_lo(dve, c)
            dve.wait_ge(small_loaded, SMALL)
            nc.vector.tensor_scalar(taps[:], taps[:], 0.5, None, ALU.mult).then_inc(taps_ready, 1)
            dve.wait_ge(count_step, 2)
            for g, window in enumerate(POOL_WINDOWS):
                half = slice(g % 2 * 64, g % 2 * 64 + 64)
                nc.vector.tensor_scalar(count[half, g // 2, :], count[half, g // 2, :], 1.0 / window, 1.0, ALU.mult,
                                        ALU.min).then_inc(count_step, 1)
            dve.wait_ge(count_step, 6)
            nc.vector.reciprocal(widen[:], count[:]).then_inc(widen_ready, 1)
            dve.wait_ge(taps_ready, 1)
            dve.wait_ge(halo_zero, 2)

            def glu(n, i):
                p = SLOT[f"ca{i}"]
                if i == 0 and not (isinstance(n, int) and n == 0):
                    for c in range(2):
                        dve.wait_ge(tap_done[c], TAPS * n)
                    nc.vector.tensor_copy(h[:, :, 0:PAD], h[:, :, TB:]).then_inc(h_halo, 1)
                    dve.wait_ge(h_halo, n)
                dve.wait_ge(proj_full, filled(n, p))
                nc.vector.scalar_tensor_tensor(out=h[:, i, PAD:], in0=sig[:, i, :], scalar=1.0, in1=proj[p % 2][:],
                                               op0=ALU.add, op1=ALU.mult).then_inc(proj_free[p % 2], 1)

            def tap(n, j):
                for i in range(2):
                    if j == 0:
                        p = SLOT[f"ca{i}"]
                        dve.wait_ge(proj_free[p % 2], earlier(n, p) + 1)
                        need(dve, conv_turned, 2 * n)
                        nc.vector.tensor_scalar(conv[:, i, :], h[:, i, 0:TB], taps[:, i, 0:1], conv_bias[:, i:i + 1],
                                                ALU.mult, ALU.add).then_inc(tap_done[i], 1)
                    else:
                        dve.wait_ge(tap_done[i], TAPS * n + j)
                        nc.vector.scalar_tensor_tensor(out=conv[:, i, :], in0=h[:, i, j:j + TB], scalar=taps[:, i, j:j + 1],
                                                       in1=conv[:, i, :], op0=ALU.mult, op1=ALU.add).then_inc(tap_done[i], 1)

            def layer_norm_stats(n):
                for s in range(SUB):
                    dve.wait_ge(conv_turned, 2 * n + s // 2 + 1)
                    nc.vector.bn_stats(stats[:, s, :], tok[s // 2][:, s % 2, :]).then_inc(stats_done, 1)
                carrier.dve_wait(dve, stats_done, SUB * n + SUB)
                for s in range(SUB):
                    nc.vector.bn_aggr(meanvar[:, s, :], stats[:, s, :]).then_inc(meanvar_done, 1)

            def layer_norm_apply(n):
                dve.wait_ge(rstd_step, 2 * n + 2)
                for s in range(SUB):
                    nc.vector.tensor_scalar(z[:, s, :], tok[s // 2][:, s % 2, :], meanvar[:, s, 0:1], ln_rstd[:, s:s + 1],
                                            ALU.subtract, ALU.mult).then_inc(z_done, 1)

            def conv_output(n, at):
                for i in range(2):
                    p = at[1] + i
                    dve.wait_ge(proj_full, filled(at[0], p))
                    if i == 0:
                        need(dve, y_conv_stored, 16 * n)
                    nc.vector.tensor_tensor(y_conv[:, i, :], proj[p % 2][:], gate_c[:, i, :], ALU.mult).then_inc(proj_free[p % 2], 1)

            def pool_output(n):
                for i in range(2):
                    p = SLOT[f"po{i}"]
                    dve.wait_ge(proj_full, filled(n, p))
                    if i == 0:
                        need(dve, y_pool_stored, 16 * n)
                    nc.vector.scalar_tensor_tensor(out=y_pool[:, i, :], in0=proj[p % 2][:], scalar=pscale[:, i:i + 1],
                                                   in1=gate_p[:, i, :], op0=ALU.mult, op1=ALU.mult).then_inc(proj_free[p % 2], 1)

            BEFORE_PW, BEFORE_PO = 8, 26

            def body(n):
                first = isinstance(n, int) and n == 0
                left = TAPS - BEFORE_PO
                for kk in range(KT):
                    st.split_lo(dve, n, kk)
                    if not first and kk < left:
                        tap(n - 1, BEFORE_PO + kk)
                if not first:
                    layer_norm_stats(n - 1)
                glu(n, 0)
                if not first:
                    layer_norm_apply(n - 1)
                glu(n, 1)
                for j in range(BEFORE_PW):
                    tap(n, j)
                if not first:
                    conv_output(n - 1, (n, SLOT["pw0"]))
                for j in range(BEFORE_PW, BEFORE_PO):
                    tap(n, j)
                pool_output(n)

            body(0)
            with dve.Fori(1, NB) as n:
                body(n)
            for j in range(BEFORE_PO, TAPS):
                tap(NB - 1, j)
            layer_norm_stats(NB - 1)
            layer_norm_apply(NB - 1)
            conv_output(NB - 1, (NB, 0))

        @block.tensor
        def _(pe):
            def project(n, name, between=None):
                p, c = SLOT[name], CHUNK_OF[name[:-1]]
                cols = slice(int(name[-1]) * P, int(name[-1]) * P + P)
                need(pe, proj_free[p % 2], earlier(n, p))
                if isinstance(n, int) and n == 0:
                    pe.wait_ge(w.lo_done, c + 1)
                for kk in range(KT):
                    if name == "cb0":
                        pe.wait_ge(st.lo_done, KT * n + kk + 1)
                    last = split3(nc, proj[p % 2][:], w.hi[:, c, kk, cols], w.lo[:, c, kk, cols], st.hi[:, kk, :],
                                  st.lo[:, kk, :], kk == 0, kk == KT - 1)
                    if between:
                        between(kk)
                last.then_inc(proj_full, 1)

            def turn_conv(n):
                for i in range(2):
                    pe.wait_ge(tap_done[i], TAPS * n + TAPS)
                for b in range(2):
                    for s in (2 * b, 2 * b + 1):
                        for i in range(2):
                            last = nc.tensor.transpose(tok[b][:, s % 2, i * P:(i + 1) * P],
                                                       conv[:, i, s * P:(s + 1) * P], st.ident[:])
                    last.then_inc(conv_turned, 1)

            def turn_z(n):
                pe.wait_ge(z_done, SUB * n + SUB)
                for i in range(2):
                    for s in range(SUB):
                        last = nc.tensor.transpose(feat[i][:, s * P:(s + 1) * P], z[:, s, i * P:(i + 1) * P], st.ident[:])
                    last.then_inc(z_turned, 1)

            def pointwise(n, at):
                pe.wait_ge(hs_done, 2 * n + 2)
                for o in range(2):
                    p = at[1] + o
                    need(pe, proj_free[p % 2], earlier(at[0], p))
                    for i in range(2):
                        last = nc.tensor.matmul(proj[p % 2][:], pw[:, i, o * P:(o + 1) * P], hs[:, i, :],
                                                start=(i == 0), stop=(i == 1))
                    last.then_inc(proj_full, 1)

            def pool_map(n):
                pe.wait_ge(diff_done, 2 * n + 2)
                for i in range(2):
                    p = SLOT[f"po{i}"]
                    need(pe, proj_free[p % 2], earlier(n, p))
                    nc.tensor.matmul(proj[p % 2][:], pool_lhs[:, i, :], diff[:, i, :], start=True, stop=True).then_inc(proj_full, 1)

            def body(n):
                first = isinstance(n, int) and n == 0
                st.transpose(pe, n, 0)
                st.transpose(pe, n, 1)
                project(n, "cb0", lambda kk: st.transpose(pe, n, kk + 2) if kk + 2 < KT else None)
                project(n, "cb1")
                if not first:
                    turn_conv(n - 1)
                project(n, "ca0")
                project(n, "ca1")
                project(n, "u0")
                if not first:
                    turn_z(n - 1)
                project(n, "u1")
                if first:
                    pe.wait_ge(small_loaded, SMALL)
                else:
                    pointwise(n - 1, (n, SLOT["pw0"]))
                for name in ("gp0", "gp1", "gc0", "gc1"):
                    project(n, name)
                pool_map(n)

            body(0)
            with pe.Fori(1, NB) as n:
                body(n)
            turn_conv(NB - 1)
            turn_z(NB - 1)
            pointwise(NB - 1, (NB, 0))


def output_phase(nc, x, w_out, final_g, y_scratch, out):
    ctx = ExitStack()
    with ctx:
        sb = lambda name, shape, dt=F32: ctx.enter_context(nc.sbuf_tensor("o_" + name, shape, dt))
        sem = lambda name: ctx.enter_context(nc.semaphore("o_" + name))
        pool_carrier = Carrier(nc, ctx, "o_pool_carrier")
        w_hi = sb("w_hi", [P, KT, D], F32R)
        w_lo = sb("w_lo", [P, KT, D], F32R)
        stage = sb("stage", [P, 2, D])
        y = sb("y", [P, KT, TB])
        y_hi = sb("y_hi", [P, 2, KT, TB], F32R)
        y_lo = sb("y_lo", [P, 2, KT, TB], F32R)
        xs = sb("xs", [P, 2, SUB, D])
        squares = sb("squares", [P, D])
        res = sb("res", [P, 2, D])
        gain = sb("gain", [P, D])
        sumsq = sb("sumsq", [P, 2, SUB])
        meansq = sb("meansq", [P, 2, SUB])
        rstd = sb("rstd", [P, 2, SUB])
        neg_half = sb("neg_half", [P, 1])
        acc = [ctx.enter_context(nc.psum_tensor(f"o_acc{b}", [P, TB], F32)) for b in range(4)]

        w_loaded = [sem("w_loaded0"), sem("w_loaded1")]
        w_hi_done = sem("w_hi_done")
        w_lo_done = sem("w_lo_done")
        gain_loaded = sem("gain_loaded")
        half_ready = sem("half_ready")
        x_loaded = [sem("x_loaded0"), sem("x_loaded1")]
        y_loaded = sem("y_loaded")
        y_hi_done = sem("y_hi_done")
        y_lo_done = sem("y_lo_done")
        acc_full = sem("acc_full")
        added = sem("added")
        squared = sem("squared")
        rstd_step = sem("rstd_step")
        finished = sem("finished")
        stored = [sem("stored0"), sem("stored1")]

        block = ctx.enter_context(nc.Block())

        @block.sync
        def _(sp):
            def load_x(n, b):
                need(sp, finished, SUB * (n - 1))
                sp.dma_start(xs[:, b], x[0, bass.ds(n * TB, TB), :].rearrange("(s p) d -> p s d", p=P)).then_inc(x_loaded[b], 16)

            def load_w(k):
                need(sp, w_lo_done, k - 1)
                dst = stage[:, k % 2, :]
                if k < Y_ATTN:
                    sp.dma_start(dst, w_out[0, k * P:(k + 1) * P, :]).then_inc(w_loaded[k % 2], 16)
                else:
                    for half in range(2):
                        row = POOL_W + CONV_W + (half * GROUP + k - Y_ATTN) * HD
                        sp.dma_start(dst[half * HD:(half + 1) * HD], w_out[0, row:row + HD, :]).then_inc(w_loaded[k % 2], 16)

            def store(n, s):
                sp.wait_ge(finished, SUB * n + s + 1)
                sp.dma_start(out[0, bass.ds(n * TB + s * P, P), :], res[:, s % 2, :]).then_inc(stored[s % 2], 16)

            for k in range(KT):
                load_w(k)
            sp.dma_start(gain[:], final_g.rearrange("(a d) -> a d", a=1).to_broadcast([P, D])).then_inc(gain_loaded, 16)
            load_x(0, 0)
            load_x(1, 1)

            def body(n, b, more):
                for s in range(SUB):
                    store(n, s)
                if more:
                    load_x(n + 2, b)

            with sp.Fori(0, NB // 2 - 1) as pair:
                body(2 * pair, 0, True)
                body(2 * pair + 1, 1, True)
            body(NB - 2, 0, False)
            body(NB - 1, 1, False)
            for b in range(2):
                sp.wait_ge(stored[b], 16 * 2 * NB)

        @block.gpsimd
        def _(pool):
            carrier = pool_carrier
            carrier.prepare(pool)
            nc.gpsimd.memset(neg_half[:], -0.5).then_inc(half_ready, 1)
            pool.wait_ge(half_ready, 1)

            def body(n, b):
                for s in range(SUB):
                    col = slice(s, s + 1)
                    carrier.pool_wait(pool, squared, SUB * n + s + 1)
                    nc.gpsimd.tensor_scalar(meansq[:, b, col], sumsq[:, b, col], 1.0 / D, EPS, ALU.mult,
                                            ALU.add).then_inc(rstd_step, 1)
                    pool.wait_ge(rstd_step, 2 * SUB * n + 2 * s + 1)
                    nc.gpsimd.tensor_tensor(rstd[:, b, col], meansq[:, b, col], neg_half[:], ALU.pow).then_inc(rstd_step, 1)

            with pool.Fori(0, NB, 2) as n:
                body(n, 0)
                body(n + 1, 1)

        @block.scalar
        def _(act):
            def load_y(n):
                need(act, y_lo_done, KT * n)
                act.dma_start(y[:], y_scratch[:, :, bass.ds(n * TB, TB)].rearrange("t p c -> p t c")).then_inc(y_loaded, 16)

            load_y(0)

            def split(n, b, k):
                act.wait_ge(y_loaded, 16 * n + 16)
                if k == 0:
                    need(act, acc_full, 8 * n - 8)
                nc.scalar.activation(y_hi[:, b, k, :], y[:, k, :], ACT.Copy).then_inc(y_hi_done, 1)

            for k in range(KT):
                split(0, 0, k)
                act.wait_ge(w_loaded[k % 2], 16 * (k // 2 + 1) if k < Y_ATTN else 16 * (2 + 2 * ((k - Y_ATTN) // 2 + 1)))
                nc.scalar.activation(w_hi[:, k, :], stage[:, k % 2, :], ACT.Copy).then_inc(w_hi_done, 1)

            def body(n, b, more):
                for s in range(SUB):
                    if more:
                        split(n + 1, 1 - b, 2 * s)
                        split(n + 1, 1 - b, 2 * s + 1)
                    act.wait_ge(added, 8 * n + 2 * s + 2)
                    if not isinstance(n, int) or n > 0 or s > 0:
                        act.wait_ge(squared, SUB * n + s)
                    nc.scalar.activation(squares[:], xs[:, b, s, :], ACT.Square,
                                         accum_out=sumsq[:, b, s:s + 1]).then_inc(squared, 1)
                if more > 1:
                    load_y(n + 2)

            load_y(1)
            body(0, 0, NB - 1)
            with act.Fori(1, NB - 3, 2) as n:
                body(n, 1, 2)
                body(n + 1, 0, 2)
            body(NB - 3, 1, 2)
            body(NB - 2, 0, 1)
            body(NB - 1, 1, 0)

        @block.vector
        def _(dve):
            def split(n, b, k):
                dve.wait_ge(y_hi_done, KT * n + k + 1)
                nc.vector.tensor_tensor(y_lo[:, b, k, :], y[:, k, :], y_hi[:, b, k, :].bitcast(F32),
                                        ALU.subtract).then_inc(y_lo_done, 1)

            for k in range(KT):
                split(0, 0, k)
                dve.wait_ge(w_hi_done, k + 1)
                nc.vector.tensor_tensor(w_lo[:, k, :], stage[:, k % 2, :], w_hi[:, k, :].bitcast(F32),
                                        ALU.subtract).then_inc(w_lo_done, 1)
            dve.wait_ge(gain_loaded, 16)

            def finish(n, b, s):
                dve.wait_ge(rstd_step, 2 * SUB * n + 2 * s + 2)
                if not isinstance(n, int) or n > 0 or s >= 2:
                    dve.wait_ge(stored[s % 2], 16 * 2 * n + 16 * (s // 2))
                nc.vector.scalar_tensor_tensor(out=res[:, s % 2, :], in0=xs[:, b, s, :], scalar=rstd[:, b, s:s + 1],
                                               in1=gain[:], op0=ALU.mult, op1=ALU.mult).then_inc(finished, 1)

            def body(n, b, more, uses):
                dve.wait_ge(x_loaded[b], uses)
                for s in range(SUB):
                    if more:
                        split(n + 1, 1 - b, 2 * s)
                        split(n + 1, 1 - b, 2 * s + 1)
                    for half in range(2):
                        cols = slice(half * TB, (half + 1) * TB)
                        dve.wait_ge(acc_full, 8 * n + 2 * s + half + 1)
                        nc.vector.tensor_tensor(xs[:, b, s, cols], acc[s % 2 * 2 + half][:], xs[:, b, s, cols],
                                                ALU.add).then_inc(added, 1)
                    if s:
                        finish(n, b, s - 1)
                finish(n, b, SUB - 1)

            body(0, 0, True, 16)
            with dve.Fori(1, NB - 1, 2) as n:
                body(n, 1, True, 8 * n + 8)
                body(n + 1, 0, True, 8 * n + 24)
            body(NB - 1, 1, False, 8 * NB)

        @block.tensor
        def _(pe):
            def body(n, b):
                for s in range(SUB):
                    toks = slice(s * P, (s + 1) * P)
                    for half in range(2):
                        cols = slice(half * TB, (half + 1) * TB)
                        bank = s % 2 * 2 + half
                        if not isinstance(n, int) or n > 0 or s >= 2:
                            pe.wait_ge(added, 8 * n + 2 * s + half - 3)
                        for k in range(KT):
                            if s == 0 and half == 0:
                                pe.wait_ge(y_lo_done, KT * n + k + 1)
                                if isinstance(n, int) and n == 0:
                                    pe.wait_ge(w_lo_done, k + 1)
                            last = split3(nc, acc[bank][:], y_hi[:, b, k, toks], y_lo[:, b, k, toks],
                                          w_hi[:, k, cols], w_lo[:, k, cols], k == 0, k == KT - 1)
                        last.then_inc(acc_full, 1)

            body(0, 0)
            with pe.Fori(1, NB - 1, 2) as n:
                body(n, 1)
                body(n + 1, 0)
            body(NB - 1, 1)


def build(nc, x, ln_g, w_in, pool_w, pool_scale, conv_dw, conv_b, conv_ln_g, conv_ln_b, conv_pw, attn_sinks,
          w_out, final_g, out):
    y_scratch = nc.dram_tensor("y_scratch", (KT, P, S), F32, kind="Internal").ap()
    attention_phase(nc, x, ln_g, w_in, attn_sinks, y_scratch)
    mixer_phase(nc, x, ln_g, w_in, pool_w, pool_scale, conv_dw, conv_b, conv_ln_g, conv_ln_b, conv_pw, y_scratch)
    output_phase(nc, x, w_out, final_g, y_scratch, out)


_INS = ["x", "ln_g", "w_in", "pool_w", "pool_scale", "conv_dw", "conv_b", "conv_ln_g", "conv_ln_b", "conv_pw",
        "attn_sinks", "w_out", "final_g"]


def kernel(**inputs):
    import numpy as _np
    import concourse.bacc as _bacc
    from concourse import mybir as _mybir
    from concourse.bass_utils import run_bass_kernel_spmd as _run

    nc = _bacc.Bacc("TRN2", target_bir_lowering=False, num_devices=1)
    arrays, args = {}, []
    for name in _INS:
        a = _np.ascontiguousarray(inputs[name])
        arrays[f"in_{name}_dram"] = a
        args.append(nc.dram_tensor(f"in_{name}_dram", a.shape, _mybir.dt.from_np(a.dtype), kind="ExternalInput").ap())
    out = nc.dram_tensor("out_dram", (1, S, D), _mybir.dt.float32, kind="ExternalOutput").ap()
    build(nc, *args, out)
    r = _run(nc, [arrays], core_ids=[0])
    return r.results[0]["out_dram"]
```

```python
from contextlib import ExitStack

import concourse.bass as bass
from concourse import mybir

F32 = mybir.dt.float32
F32R = mybir.dt.float32r
ALU = mybir.AluOpType
ACT = mybir.ActivationFunctionType

P = 128
D = 1024
S = 4096
KT = D // P
TB = 512
NB = S // TB
SUB = TB // P
POOL_W = 256
CONV_W = 256
TAPS = 31
HEADS = 8
KV = 2
GROUP = HEADS // KV
HD = 64
ATTN_W = HEADS * HD
WINDOW = 128
EPS = 1e-6
MASKED = -1e30
CHUNK = 256
POOL_WINDOWS = (2, 4, 8, 16)
HALO = 16
TURNS = 4
PAD = TAPS - 1

COL_U = 0
COL_GP = COL_U + POOL_W
COL_CA = COL_GP + POOL_W
COL_CB = COL_CA + CONV_W
COL_GC = COL_CB + CONV_W
COL_Q = COL_GC + CONV_W
COL_K = COL_Q + ATTN_W
COL_V = COL_K + KV * HD
COL_GA = COL_V + KV * HD

Y_POOL, Y_CONV, Y_ATTN = 0, 2, 4


def need(engine, sem, count):
    if not isinstance(count, int) or count > 0:
        engine.wait_ge(sem, count)


class Carrier:

    def __init__(self, nc, ctx, name):
        self.nc = nc
        self.cell = ctx.enter_context(nc.sbuf_tensor(name, [P, 2], F32))
        self.ready = ctx.enter_context(nc.semaphore(name + "_ready"))

    def prepare(self, engine):
        engine.memset(self.cell[:], 0.0).then_inc(self.ready, 1)
        engine.wait_ge(self.ready, 1)

    def dve_wait(self, dve, sem, count):
        dve.wait_ge(sem, count)
        if not isinstance(count, int):
            self.nc.vector.tensor_copy(self.cell[:, 0:1], self.cell[:, 1:2])

    def pool_wait(self, pool, sem, count):
        pool.wait_ge(sem, count)
        if not isinstance(count, int):
            self.nc.gpsimd.tensor_tensor(self.cell[:, 0:1], self.cell[:, 1:2], self.cell[:, 1:2], ALU.add)


def identity(nc, pool, ident, sem):
    nc.gpsimd.memset(ident[:], 0.0).then_inc(sem, 1)
    pool.wait_ge(sem, 1)
    nc.gpsimd.affine_select(out=ident[:], in_=ident[:], compare_op=ALU.not_equal, fill=1.0,
                            base=0, pattern=[[-1, P]], channel_multiplier=1).then_inc(sem, 1)


class XStage:

    def __init__(self, nc, ctx, x, ln_g, turn, squares, tag):
        self.nc, self.x, self.ln_g, self.turn = nc, x, ln_g, turn
        sb = lambda name, shape, dt=F32: ctx.enter_context(nc.sbuf_tensor(tag + name, shape, dt))
        sem = lambda name: ctx.enter_context(nc.semaphore(tag + name))
        self.xs = sb("xs", [P, SUB, D])
        self.squares = squares
        self.sumsq = sb("sumsq", [P, SUB])
        self.meansq = sb("meansq", [P, SUB])
        self.rstd = sb("rstd", [P, SUB])
        self.neg_half = sb("neg_half", [P, SUB])
        self.gain = sb("gain", [P, KT])
        self.ident = sb("ident", [P, P])
        self.hi = sb("xT_hi", [P, KT, TB], F32R)
        self.lo = sb("xT_lo", [P, KT, TB], F32R)
        self.loaded = [sem(f"x_loaded{s}") for s in range(SUB)]
        self.gain_loaded = sem("gain_loaded")
        self.ident_ready = sem("ident_ready")
        self.half_ready = sem("half_ready")
        self.squared = sem("x_squared")
        self.rstd_steps = sem("rstd_steps")
        self.scaled = sem("x_scaled")
        self.turned = sem("x_turned")
        self.hi_done = sem("xT_hi_done")
        self.lo_done = sem("xT_lo_done")

    def load(self, sp, n):
        need(sp, self.turned, KT * n)
        for s in range(SUB):
            sp.dma_start(self.xs[:, s, :], self.x[0, bass.ds(n * TB + s * P, P), :]).then_inc(self.loaded[s], 16)

    def load_gain(self, sp):
        with self.nc.allow_non_contiguous_dma(reason="1024 values, once"):
            sp.dma_start(self.gain[:], self.ln_g[0].rearrange("(k p) -> p k", p=P)).then_inc(self.gain_loaded, 16)

    def square(self, act, n):
        for s in range(SUB):
            act.wait_ge(self.loaded[s], 16 * n + 16)
            if not isinstance(n, int) or n > 0 or s > 0:
                act.wait_ge(self.squared, SUB * n + s)
            self.nc.scalar.activation(self.squares[:], self.xs[:, s, :], ACT.Square,
                                      accum_out=self.sumsq[:, s:s + 1]).then_inc(self.squared, 1)

    def prepare(self, pool, carrier):
        self.carrier = carrier
        self.nc.gpsimd.memset(self.neg_half[:], -0.5).then_inc(self.half_ready, 1)
        identity(self.nc, pool, self.ident, self.ident_ready)
        pool.wait_ge(self.half_ready, 1)

    def scale(self, pool, n):
        nc = self.nc
        self.carrier.pool_wait(pool, self.squared, SUB * n + SUB)
        nc.gpsimd.tensor_scalar(self.meansq[:], self.sumsq[:], 1.0 / D, EPS, ALU.mult, ALU.add).then_inc(self.rstd_steps, 1)
        pool.wait_ge(self.rstd_steps, 2 * n + 1)
        nc.gpsimd.tensor_tensor(self.rstd[:], self.meansq[:], self.neg_half[:], ALU.pow).then_inc(self.rstd_steps, 1)
        self.carrier.pool_wait(pool, self.rstd_steps, 2 * n + 2)
        for s in range(SUB):
            nc.gpsimd.tensor_scalar(self.xs[:, s, :], self.xs[:, s, :], self.rstd[:, s:s + 1], 1.0,
                                    ALU.mult, ALU.mult).then_inc(self.scaled, 1)

    def transpose(self, pe, n, k):
        if k == 0:
            pe.wait_ge(self.scaled, SUB * n + SUB)
            if isinstance(n, int) and n == 0:
                pe.wait_ge(self.ident_ready, 2)
        if k >= TURNS:
            pe.wait_ge(self.lo_done, KT * n + k - TURNS + 1)
        for s in range(SUB):
            last = self.nc.tensor.transpose(self.turn[k % TURNS][:, s * P:(s + 1) * P],
                                            self.xs[:, s, k * P:(k + 1) * P], self.ident[:])
        last.then_inc(self.turned, 1)

    def split_hi(self, act, n, k):
        if isinstance(n, int) and n == 0 and k == 0:
            act.wait_ge(self.gain_loaded, 16)
        act.wait_ge(self.turned, KT * n + k + 1)
        self.nc.scalar.activation(self.hi[:, k, :], self.turn[k % TURNS][:], ACT.Copy,
                                  scale=self.gain[:, k:k + 1]).then_inc(self.hi_done, 1)

    def split_lo(self, dve, n, k):
        dve.wait_ge(self.hi_done, KT * n + k + 1)
        self.nc.vector.scalar_tensor_tensor(out=self.lo[:, k, :], in0=self.turn[k % TURNS][:],
                                            scalar=self.gain[:, k:k + 1], in1=self.hi[:, k, :].bitcast(F32),
                                            op0=ALU.mult, op1=ALU.subtract).then_inc(self.lo_done, 1)


def split3(nc, out, w_hi, w_lo, x_hi, x_lo, first, last):
    nc.tensor.matmul(out, w_hi, x_hi, start=first, stop=False)
    nc.tensor.matmul(out, w_lo, x_hi, start=False, stop=False)
    return nc.tensor.matmul(out, w_hi, x_lo, start=False, stop=last)


class Weights:

    def __init__(self, nc, ctx, w_in, cols, stage, tag):
        self.nc, self.w_in, self.cols, self.stage = nc, w_in, cols, stage
        n = len(cols)
        self.hi = ctx.enter_context(nc.sbuf_tensor(tag + "w_hi", [P, n, KT, CHUNK], F32R))
        self.lo = ctx.enter_context(nc.sbuf_tensor(tag + "w_lo", [P, n, KT, CHUNK], F32R))
        sem = lambda name: ctx.enter_context(nc.semaphore(tag + name))
        self.loaded = [sem("w_loaded0"), sem("w_loaded1")]
        self.hi_done = sem("w_hi_done")
        self.lo_done = sem("w_lo_done")

    def load(self, sp, c):
        need(sp, self.lo_done, c - 1)
        col = self.cols[c]
        firsts = [col, col + P] if isinstance(col, int) else [col[0] + col[1] * P, col[0] + GROUP * HD + col[1] * P]
        for half, first in enumerate(firsts):
            sp.dma_start(self.stage[c % 2][:, :, half * P:(half + 1) * P],
                         self.w_in[0, :, first:first + P].rearrange("(k p) c -> p k c", p=P)).then_inc(self.loaded[c % 2], 16)

    def parts(self, c, whole):
        staged = self.stage[c % 2]
        if isinstance(self.cols[c], int):
            return [(staged, whole[:, c])]
        heads = lambda t: staged.rearrange("p k (s t d) -> p k s t d", s=KV, t=2)[:, :, :, t, :]
        tile = lambda t: whole[:, c, :, t * P:(t + 1) * P].rearrange("p k (s d) -> p k s d", s=KV)
        return [(heads(t), tile(t)) for t in range(2)]

    def split_hi(self, act, c):
        act.wait_ge(self.loaded[c % 2], 32 * (c // 2) + 32)
        for staged, hi in self.parts(c, self.hi):
            last = self.nc.scalar.activation(hi, staged, ACT.Copy)
        last.then_inc(self.hi_done, 1)

    def split_lo(self, dve, c):
        dve.wait_ge(self.hi_done, c + 1)
        for (staged, lo), (_, hi) in zip(self.parts(c, self.lo), self.parts(c, self.hi)):
            last = self.nc.vector.tensor_tensor(lo, staged, hi.bitcast(F32), ALU.subtract)
        last.then_inc(self.lo_done, 1)


def attention_phase(nc, x, ln_g, w_in, attn_sinks, y_scratch):
    ctx = ExitStack()
    with ctx:
        sb = lambda name, shape, dt=F32: ctx.enter_context(nc.sbuf_tensor("a_" + name, shape, dt))
        sem = lambda name: ctx.enter_context(nc.semaphore("a_" + name))
        pool_carrier = Carrier(nc, ctx, "a_pool_carrier")
        dve_carrier = Carrier(nc, ctx, "a_dve_carrier")
        bank = lambda name, shape: ctx.enter_context(nc.psum_tensor("a_" + name, shape, F32))
        proj = [bank(f"proj{b}", [P, TB]) for b in range(2)]
        score = [bank(f"score{b}", [P, 2, 2 * P]) for b in range(4)]
        turn = [bank(f"turn{b}", [P, TB]) for b in range(2)]
        tanh = sb("tanh", [P, 2, TB])
        st = XStage(nc, ctx, x, ln_g, turn + [score[b].rearrange("p a b -> p (a b)") for b in (2, 3)],
                    tanh.rearrange("p a b -> p (a b)"), "a_")
        probs = sb("probs", [P, 2, HEADS, 2 * P])
        stage = [probs[:, b].rearrange("p h j -> p (h j)").rearrange("p (k c) -> p k c", k=KT) for b in range(2)]
        w = Weights(nc, ctx, w_in, [COL_K, (COL_Q, 0), (COL_Q, 1), (COL_GA, 0), (COL_GA, 1)], stage, "a_")

        q = sb("q", [P, HEADS, TB], F32R)
        k_hi = sb("k_hi", [P, KV, P + TB], F32R)
        k_lo = sb("k_lo", [P, P + TB], F32R)
        vT = tanh[:, 0]
        v = sb("v", [P, 1 + SUB, P])
        gate = sb("gate", [P, GROUP, TB])
        dist = gate[:, GROUP - 1, 0:2 * P]
        pT = sb("pT", [P, 2, KV, GROUP * P])
        y = sb("y", [P, GROUP, TB])
        bias = sb("bias", [P, HEADS, 2 * P])
        sinks = sb("sinks", [P, HEADS])
        rowmax = sb("rowmax", [P, 2, HEADS])
        negmax = sb("negmax", [P, 2, HEADS])
        sinkdiff = sb("sinkdiff", [P, 2, HEADS])
        sinkexp = sb("sinkexp", [P, 2, HEADS])
        rowsum = sb("rowsum", [P, 2, HEADS])
        denom = sb("denom", [P, 2, HEADS])
        inv = sb("inv", [P, 2, HEADS])
        neg_one = sb("neg_one", [P, HEADS])

        consts = sem("consts")
        halo_zero = sem("halo_zero")
        sinks_loaded = sem("sinks_loaded")
        bias_ready = sem("bias_ready")
        bias_step = sem("bias_step")
        proj_full = sem("proj_full")
        proj_free = [sem("proj_free0"), sem("proj_free1")]
        k_halo = sem("k_halo")
        k_lo_halo = sem("k_lo_halo")
        k_hi_done = sem("k_hi_done")
        q_hi_done = sem("q_hi_done")
        v_halo = sem("v_halo")
        v_turned = sem("v_turned")
        v_ready = sem("v_ready")
        score_full = sem("score_full")
        score_taken = sem("score_taken")
        row_step = sem("row_step")
        max_ready = sem("max_ready")
        sink_done = sem("sink_done")
        exp_done = sem("exp_done")
        den_step = sem("den_step")
        probs_ready = sem("probs_ready")
        p_turned = sem("p_turned")
        pT_act = sem("pT_act")
        pT_dve = sem("pT_dve")
        tanh_done = sem("tanh_done")
        gated = sem("gated")
        y_stored = sem("y_stored")

        SLOT = {name: p for p, name in enumerate(
            ["k", "q0", "o3", "q1", "q2", "q3", "v", "g0", "g1", "o0", "g2", "o1", "g3", "o2"])}
        USES = len(SLOT)

        def early(n, p):
            return isinstance(n, int) and n == 0 and p < SLOT["o3"]

        def filled(n, p):
            return USES * n + p + (1 if early(n, p) else 0)

        def earlier(n, p):
            return USES // 2 * n + p // 2 - (0 if p % 2 or early(n, p) else 1)

        def slot(name):
            return SLOT[name]

        halves = [slice(0, HD), slice(HD, P)]

        block = ctx.enter_context(nc.Block())

        @block.sync
        def _(sp):
            st.load(sp, 0)
            w.load(sp, 0)
            st.load_gain(sp)
            sp.dma_start(sinks[:], attn_sinks[0:1, :].to_broadcast([P, HEADS])).then_inc(sinks_loaded, 16)
            for c in range(1, 5):
                w.load(sp, c)

            def store(n):
                sp.wait_ge(gated, n + 1)
                sp.dma_start(y_scratch[Y_ATTN:Y_ATTN + GROUP, :, bass.ds(n * TB, TB)].rearrange("t p c -> p t c"),
                             y[:]).then_inc(y_stored, 16)

            st.load(sp, 1)
            with sp.Fori(1, NB - 1) as n:
                st.load(sp, n + 1)
                store(n - 1)
            store(NB - 2)
            store(NB - 1)
            sp.wait_ge(y_stored, 16 * NB)

        @block.gpsimd
        def _(pool):
            carrier = pool_carrier
            carrier.prepare(pool)
            nc.gpsimd.iota(dist[:], pattern=[[-1, 2 * P]], base=P, channel_multiplier=1,
                           allow_small_or_imprecise_dtypes=True).then_inc(bias_step, 1)
            nc.gpsimd.memset(neg_one[:], -1.0).then_inc(consts, 1)
            st.prepare(pool, carrier)
            st.scale(pool, 0)
            pool.wait_ge(bias_step, 1)
            pool.wait_ge(consts, 1)

            def alibi(lo, hi, steps):
                for h in range(HEADS):
                    last = nc.gpsimd.tensor_scalar(bias[:, h, lo:hi], dist[:, lo:hi], -(2.0 ** (-8.0 * (h + 1) / HEADS)),
                                                   1.0, ALU.mult, ALU.mult)
                last.then_inc(bias_step, 1)
                pool.wait_ge(bias_step, steps + 1)
                part = bias[:, :, lo:hi]
                nc.gpsimd.affine_select(out=part, in_=part, compare_op=ALU.is_ge, fill=MASKED, base=P - lo,
                                        pattern=[[0, HEADS], [-1, hi - lo]], channel_multiplier=1).then_inc(bias_step, 1)
                pool.wait_ge(bias_step, steps + 2)
                nc.gpsimd.affine_select(out=part, in_=part, compare_op=ALU.is_ge, fill=MASKED, base=WINDOW - 1 - P + lo,
                                        pattern=[[0, HEADS], [1, hi - lo]], channel_multiplier=-1).then_inc(bias_ready, 1)

            nc.gpsimd.memset(bias[:, :, 0:P], MASKED).then_inc(consts, 1)
            pool.wait_ge(consts, 2)
            alibi(P, 2 * P, 1)

            def normalise(n, j):
                m, b = 4 * n + j, j % 2
                for kv in range(KV):
                    heads = slice(kv * GROUP, (kv + 1) * GROUP)
                    pool.wait_ge(exp_done, 2 * m + kv + 1)
                    nc.gpsimd.tensor_tensor(denom[:, b, heads], rowsum[:, b, heads], sinkexp[:, b, heads],
                                            ALU.add).then_inc(den_step, 1)
                    pool.wait_ge(den_step, 4 * m + 2 * kv + 1)
                    nc.gpsimd.tensor_tensor(inv[:, b, heads], denom[:, b, heads], neg_one[:, heads],
                                            ALU.pow).then_inc(den_step, 1)
                    carrier.pool_wait(pool, den_step, 4 * m + 2 * kv + 2)
                    for t in range(GROUP):
                        h = kv * GROUP + t
                        last = nc.gpsimd.tensor_scalar(probs[:, b, h, :], probs[:, b, h, :], inv[:, b, h:h + 1], 0.5,
                                                       ALU.mult, ALU.mult)
                    last.then_inc(probs_ready, 1)

            def gate_output(n, at):
                pool.wait_ge(proj_free[at[1] % 2], earlier(*at) + 1)
                for t in range(GROUP):
                    last = nc.gpsimd.tensor_tensor(y[:, t, :], y[:, t, :], gate[:, t, :], ALU.mult)
                last.then_inc(gated, 1)

            def body(n, more):
                if not isinstance(n, int) or n > 0:
                    gate_output(n - 1, (n, slot("o3")))
                if more:
                    st.scale(pool, n + 1)
                if isinstance(n, int) and n == 0:
                    pool.wait_ge(score_taken, 2)
                    alibi(0, P, 3)
                for j in range(SUB):
                    normalise(n, j)

            body(0, True)
            with pool.Fori(1, NB - 1) as n:
                body(n, True)
            body(NB - 1, False)
            gate_output(NB - 1, (NB, 0))

        @block.scalar
        def _(act):
            st.square(act, 0)
            for c in range(5):
                w.split_hi(act, c)

            def copy_out(n, p, out):
                act.wait_ge(proj_full, filled(n, p))
                nc.scalar.activation(out, proj[p % 2][:], ACT.Copy).then_inc(proj_free[p % 2], 1)

            def q_hi(n, t):
                p = slot(f"q{t}")
                act.wait_ge(proj_full, filled(n, p))
                for kv in range(KV):
                    last = nc.scalar.activation(q[halves[kv], kv * GROUP + t, :], proj[p % 2][halves[kv], :], ACT.Copy,
                                                scale=HD ** -0.5)
                last.then_inc(q_hi_done, 1)

            def exps(n, j, kv):
                m, b = 4 * n + j, j % 2
                heads = slice(kv * GROUP, (kv + 1) * GROUP)
                act.wait_ge(max_ready, 2 * m + kv + 1)
                nc.scalar.activation(sinkexp[:, b, heads], sinkdiff[:, b, heads], ACT.Exp)
                for t in range(GROUP):
                    h = kv * GROUP + t
                    last = nc.scalar.activation(probs[:, b, h, :], probs[:, b, h, :], ACT.Exp,
                                                bias=negmax[:, b, h:h + 1], accum_out=rowsum[:, b, h:h + 1])
                last.then_inc(exp_done, 1)

            def pT_copy(m, kv):
                act.wait_ge(p_turned, 4 * m + 2 * kv + 1)
                nc.scalar.activation(pT[:, 0, kv, :], st.turn[0][:], ACT.Copy).then_inc(pT_act, 1)

            def gate_tanh(n, t):
                p = slot(f"g{t}")
                act.wait_ge(proj_full, filled(n, p))
                nc.scalar.activation(tanh[:, t % 2, :], proj[p % 2][:], ACT.Tanh, scale=0.5).then_inc(tanh_done, 1)

            def body(n, more):
                first = isinstance(n, int) and n == 0
                for kk in range(KT):
                    st.split_hi(act, n, kk)
                act.wait_ge(proj_full, filled(n, slot("k")))
                if first:
                    act.wait_ge(halo_zero, 3)
                else:
                    nc.scalar.activation(k_hi[:, :, 0:P], k_hi[:, :, TB:TB + P], ACT.Copy).then_inc(k_halo, 1)
                    act.wait_ge(k_halo, n)
                for kv in range(KV):
                    for rows in halves:
                        last = nc.scalar.activation(k_hi[rows, kv, P:], proj[slot("k") % 2][halves[kv], :], ACT.Copy)
                last.then_inc(k_hi_done, 1)
                if not first:
                    pT_copy(4 * n - 1, 0)
                    pT_copy(4 * n - 1, 1)
                q_hi(n, 0)
                q_hi(n, 1)
                if more:
                    st.square(act, n + 1)
                q_hi(n, 2)
                q_hi(n, 3)
                act.wait_ge(st.squared, SUB * (n + 2) if more else SUB * NB)
                copy_out(n, slot("v"), vT)
                act.wait_ge(v_turned, n + 1)
                if not first:
                    nc.scalar.activation(v[:, 0, :], v[:, SUB, :], ACT.Copy).then_inc(v_halo, 1)
                    act.wait_ge(v_halo, n)
                nc.scalar.activation(v[:, 1:, :].rearrange("p a d -> p (a d)"), turn[1][:], ACT.Copy).then_inc(v_ready, 1)
                for j in range(SUB):
                    if j > 1:
                        pT_copy(4 * n + j - 1, 0)
                    exps(n, j, 0)
                    if j == 1:
                        pT_copy(4 * n + j - 1, 0)
                    exps(n, j, 1)
                    if j:
                        pT_copy(4 * n + j - 1, 1)
                    gate_tanh(n, j)

            body(0, True)
            with act.Fori(1, NB - 1) as n:
                body(n, True)
            body(NB - 1, False)
            pT_copy(4 * NB - 1, 0)
            pT_copy(4 * NB - 1, 1)

        @block.vector
        def _(dve):
            carrier = dve_carrier
            carrier.prepare(dve)
            for part in (k_hi[:, :, 0:P], k_lo[:, 0:P]):
                nc.vector.memset(part.bitcast(F32), 0.0).then_inc(halo_zero, 1)
            nc.vector.memset(v[:, 0, :], 0.0).then_inc(halo_zero, 1)
            for c in range(5):
                w.split_lo(dve, c)
            dve.wait_ge(sinks_loaded, 16)

            def take_scores(n, j, kv):
                m, b = 4 * n + j, j % 2
                if isinstance(n, int) and n == 0 and kv == 0:
                    dve.wait_ge(bias_ready, 1 if j == 0 else 2)
                heads = slice(kv * GROUP, (kv + 1) * GROUP)
                carrier.dve_wait(dve, score_full, 2 * m + kv + 1)
                for h in range(kv * GROUP, (kv + 1) * GROUP):
                    last = nc.vector.tensor_tensor_reduce(
                        out=probs[:, b, h, :], in0=score[h // 2][:, h % 2, :], in1=bias[:, h, :], scale=1.0,
                        scalar=sinks[:, h:h + 1], op0=ALU.add, op1=ALU.max, accum_out=rowmax[:, b, h:h + 1])
                last.then_inc(score_taken, 1)
                dve.wait_ge(score_taken, 2 * m + kv + 1)
                nc.vector.tensor_scalar(negmax[:, b, heads], rowmax[:, b, heads], -1.0, None, ALU.mult).then_inc(row_step, 1)
                nc.vector.tensor_tensor(sinkdiff[:, b, heads], sinks[:, heads], rowmax[:, b, heads],
                                        ALU.subtract).then_inc(max_ready, 1)

            def pT_copy(m, kv):
                dve.wait_ge(p_turned, 4 * m + 2 * kv + 2)
                nc.vector.tensor_copy(pT[:, 1, kv, :], st.turn[1][:]).then_inc(pT_dve, 1)

            def make_k_lo(n):
                p = slot("k")
                if not isinstance(n, int) or n > 0:
                    dve.wait_ge(proj_full, filled(n, p))
                    nc.vector.tensor_copy(k_lo[:, 0:P], k_lo[:, TB:TB + P]).then_inc(k_lo_halo, 1)
                    dve.wait_ge(k_lo_halo, n)
                dve.wait_ge(k_hi_done, n + 1)
                for kv in range(KV):
                    last = nc.vector.tensor_tensor(k_lo[halves[kv], P:], proj[p % 2][halves[kv], :],
                                                   k_hi[halves[kv], kv, P:].bitcast(F32), ALU.subtract)
                last.then_inc(proj_free[p % 2], 1)

            def make_q_lo(n, t):
                p = slot(f"q{t}")
                dve.wait_ge(q_hi_done, GROUP * n + t + 1)
                for kv in range(KV):
                    last = nc.vector.scalar_tensor_tensor(
                        out=q[halves[1 - kv], kv * GROUP + t, :], in0=proj[p % 2][halves[kv], :], scalar=HD ** -0.5,
                        in1=q[halves[kv], kv * GROUP + t, :].bitcast(F32), op0=ALU.mult, op1=ALU.subtract)
                last.then_inc(proj_free[p % 2], 1)

            def gate_make(n, t):
                p = slot(f"g{t}")
                if t == 0:
                    need(dve, gated, n)
                dve.wait_ge(tanh_done, GROUP * n + t + 1)
                nc.vector.scalar_tensor_tensor(out=gate[:, t, :], in0=tanh[:, t % 2, :], scalar=1.0, in1=proj[p % 2][:],
                                               op0=ALU.add, op1=ALU.mult).then_inc(proj_free[p % 2], 1)

            def output(n, j, at):
                dve.wait_ge(proj_full, filled(*at))
                if j == 0:
                    need(dve, y_stored, 16 * n)
                nc.vector.tensor_copy(y[:, :, j * P:(j + 1) * P],
                                      proj[at[1] % 2][:].rearrange("p (t c) -> p t c", t=GROUP)).then_inc(proj_free[at[1] % 2], 1)

            def body(n):
                first = isinstance(n, int) and n == 0
                for kk in range(KT):
                    st.split_lo(dve, n, kk)
                make_k_lo(n)
                if not first:
                    pT_copy(4 * n - 1, 0)
                    pT_copy(4 * n - 1, 1)
                make_q_lo(n, 0)
                if not first:
                    output(n - 1, 3, (n, slot("o3")))
                for t in range(1, GROUP):
                    make_q_lo(n, t)
                for j in range(SUB):
                    for kv in range(KV):
                        take_scores(n, j, kv)
                        if kv == 0 and j > 1:
                            pT_copy(4 * n + j - 1, 0)
                    if j == 1:
                        pT_copy(4 * n + j - 1, 0)
                    if j:
                        pT_copy(4 * n + j - 1, 1)
                    gate_make(n, j)
                    if j:
                        output(n, j - 1, (n, slot(f"o{j - 1}")))

            body(0)
            with dve.Fori(1, NB) as n:
                body(n)
            pT_copy(4 * NB - 1, 0)
            pT_copy(4 * NB - 1, 1)
            output(NB - 1, 3, (NB, 0))

        @block.tensor
        def _(pe):
            def weight(name):
                c, half = (0, "kv".index(name)) if name in "kv" else (1 + 2 * (name[0] == "g") + int(name[1]) // 2, int(name[1]) % 2)
                return lambda part, kk: part[:, c, kk, half * P:(half + 1) * P]

            def project(n, name, between=None):
                p = slot(name)
                wt = weight(name)
                need(pe, proj_free[p % 2], earlier(n, p))
                if isinstance(n, int) and n == 0:
                    pe.wait_ge(w.lo_done, {"k": 1, "v": 1, "q": 3, "g": 5}[name[0]])
                for kk in range(KT):
                    if name == "k":
                        pe.wait_ge(st.lo_done, KT * n + kk + 1)
                    last = split3(nc, proj[p % 2][:], wt(w.hi, kk), wt(w.lo, kk), st.hi[:, kk, :], st.lo[:, kk, :],
                                  kk == 0, kk == KT - 1)
                    if between and kk < KT - 1:
                        between(kk)
                last.then_inc(proj_full, 1)

            def scores(n, j):
                m = 4 * n + j
                keys = slice(j * P, (j + 2) * P)
                for kv in range(KV):
                    need(pe, score_taken, 2 * (m - 1) + kv + 1)
                    rows = halves[kv]
                    for h in range(kv * GROUP, (kv + 1) * GROUP):
                        out, queries = score[h // 2][:, h % 2, :], q[:, h, j * P:(j + 1) * P]
                        nc.tensor.matmul(out, queries, k_hi[:, kv, keys], start=True, stop=False)
                        last = nc.tensor.matmul(out, queries[rows], k_lo[rows, keys], start=False, stop=True)
                    last.then_inc(score_full, 1)

            def turn_probs(m, j, kv):
                for kt in range(2):
                    pe.wait_ge(probs_ready, 2 * m + kv + 1)
                    if kv == 1:
                        pe.wait_ge(pT_dve if kt else pT_act, 2 * m + 1)
                    for t in range(GROUP):
                        last = nc.tensor.transpose(st.turn[kt][:, t * P:(t + 1) * P],
                                                   probs[:, j % 2, kv * GROUP + t, kt * P:(kt + 1) * P], st.ident[:])
                    last.then_inc(p_turned, 1)

            def turning(m, j, at):
                return lambda kk: turn_probs(m, j, at.index(kk)) if kk in at else None

            def attend(m, j, at):
                p = at[1]
                need(pe, proj_free[p % 2], earlier(*at))
                pe.wait_ge(pT_act, 2 * m + 2)
                pe.wait_ge(pT_dve, 2 * m + 2)
                for kt in range(2):
                    for kv in range(KV):
                        rows = slice(kv * HD, (kv + 1) * HD)
                        last = nc.tensor.matmul(proj[p % 2][rows, :], v[:, j + kt, rows], pT[:, kt, kv, :],
                                                start=(kt == 0), stop=(kt == 1))
                last.then_inc(proj_full, 1)

            def body(n):
                first = isinstance(n, int) and n == 0
                for kk in range(TURNS):
                    st.transpose(pe, n, kk)
                project(n, "k", lambda kk: st.transpose(pe, n, kk + TURNS) if kk + TURNS < KT else None)
                if first:
                    project(n, "q0")
                else:
                    project(n, "q0", turning(4 * n - 1, 3, (3, 5)))
                    attend(4 * n - 1, 3, (n, slot("o3")))
                for name in ("q1", "q2", "q3", "v"):
                    project(n, name)
                for name in ("q2", "q3"):
                    pe.wait_ge(proj_free[slot(name) % 2], earlier(n, slot(name)) + 1)

                def turn_v(kk):
                    if kk == 2:
                        pe.wait_ge(proj_free[slot("v") % 2], earlier(n, slot("v")) + 1)
                        for s in range(SUB):
                            last = nc.tensor.transpose(turn[1][:, s * P:(s + 1) * P], vT[:, s * P:(s + 1) * P], st.ident[:])
                        last.then_inc(v_turned, 1)

                for j in range(SUB):
                    scores(n, j)
                    if j == 0:
                        project(n, "g0", turn_v)
                        pe.wait_ge(v_ready, n + 1)
                    else:
                        m = 4 * n + j - 1
                        project(n, f"g{j}", turning(m, j - 1, (3, 6) if j == 1 else (0, 3)))
                        attend(m, j - 1, (n, slot(f"o{j - 1}")))

            body(0)
            with pe.Fori(1, NB) as n:
                body(n)
            for kv in range(KV):
                turn_probs(4 * NB - 1, 3, kv)
            attend(4 * NB - 1, 3, (NB, 0))


def mixer_phase(nc, x, ln_g, w_in, pool_w, pool_scale, conv_dw, conv_b, conv_ln_g, conv_ln_b, conv_pw, y_scratch):
    ctx = ExitStack()
    with ctx:
        sb = lambda name, shape, dt=F32: ctx.enter_context(nc.sbuf_tensor("m_" + name, shape, dt))
        sem = lambda name: ctx.enter_context(nc.semaphore("m_" + name))
        pool_carrier = Carrier(nc, ctx, "m_pool_carrier")
        dve_carrier = Carrier(nc, ctx, "m_dve_carrier")
        bank = lambda name, shape: ctx.enter_context(nc.psum_tensor("m_" + name, shape, F32))
        proj = [bank(f"proj{b}", [P, TB]) for b in range(2)]
        tok = [bank(f"tok{b}", [P, 2, CONV_W]) for b in range(2)]
        feat = [bank(f"feat{b}", [P, TB]) for b in range(2)]
        st = XStage(nc, ctx, x, ln_g, [bank(f"turn{b}", [P, TB]) for b in range(2)] + feat, sb("squares", [P, D]), "m_")
        stage_buf = sb("stage", [P, 2, KT, CHUNK])
        w = Weights(nc, ctx, w_in, [COL_CB, COL_CA, COL_U, COL_GP, COL_GC], [stage_buf[:, 0], stage_buf[:, 1]], "m_")
        CHUNK_OF = {"cb": 0, "ca": 1, "u": 2, "gp": 3, "gc": 4}

        sig = sb("sig", [P, 2, TB])
        h = sb("h", [P, 2, PAD + TB])
        conv = sb("conv", [P, 2, TB])
        taps = sb("taps", [P, 2, TAPS])
        conv_bias = sb("conv_bias", [P, 2])
        ln_gain = sb("ln_gain", [P, 2])
        ln_bias = sb("ln_bias", [P, 2])
        stats = sb("stats", [P, SUB, 6])
        meanvar = sb("meanvar", [P, SUB, 2])
        var_eps = sb("var_eps", [P, SUB])
        ln_rstd = sb("ln_rstd", [P, SUB])
        neg_mean = sb("neg_mean", [P, SUB])
        ln_shift = sb("ln_shift", [P, SUB])
        z = sb("z", [P, SUB, CONV_W])
        hs = sb("hs", [P, 2, TB])
        pw = sb("pw", [P, 2, CONV_W])
        u = sb("u", [P, 2, HALO + TB])
        sums = sb("sums", [P, 2, 2, HALO + TB])
        diff = sb("diff", [P, 2, TB])
        count = sb("count", [P, 2, HALO])
        widen = sb("widen", [P, 2, HALO])
        pool_lhs = sb("pool_lhs", [P, 2, P])
        pscale = sb("pscale", [P, 2, P])
        pool_map = sb("pool_map", [P, 2, P])
        gate_p = sb("gate_p", [P, 2, TB])
        gate_c = sb("gate_c", [P, 2, TB])
        y_pool = sb("y_pool", [P, 2, TB])
        y_conv = sb("y_conv", [P, 2, TB])

        small_loaded = sem("small_loaded")
        pool_w_zero = sem("pool_w_zero")
        halo_zero = sem("halo_zero")
        taps_ready = sem("taps_ready")
        pool_lhs_ready = sem("pool_lhs_ready")
        count_step = sem("count_step")
        widen_ready = sem("widen_ready")
        sums_done = sem("sums_done")
        means_done = sem("means_done")
        proj_full = sem("proj_full")
        proj_free = [sem("proj_free0"), sem("proj_free1")]
        h_halo = [sem("h_halo0"), sem("h_halo1")]
        h_ready = sem("h_ready")
        tap_done = [sem("tap_done0"), sem("tap_done1")]
        conv_turned = sem("conv_turned")
        stats_done = sem("stats_done")
        meanvar_done = sem("meanvar_done")
        rstd_step = sem("rstd_step")
        z_done = sem("z_done")
        z_turned = sem("z_turned")
        hs_done = sem("hs_done")
        u_halo = sem("u_halo")
        pool_step = sem("pool_step")
        diff_done = sem("diff_done")
        y_pool_done = sem("y_pool_done")
        y_conv_done = sem("y_conv_done")
        y_pool_stored = sem("y_pool_stored")
        y_conv_stored = sem("y_conv_stored")

        SLOT = {name: p for p, name in enumerate(
            ["cb0", "ca0", "cb1", "ca1", "u0", "u1", "pw0", "pw1", "gp0", "gp1", "gc0", "gc1", "po0", "po1"])}
        USES = len(SLOT)

        def early(n, p):
            return isinstance(n, int) and n == 0 and p < SLOT["pw0"]

        def filled(n, p):
            return USES * n + p + 1 - (0 if early(n, p) else 2)

        def earlier(n, p):
            return USES // 2 * n + p // 2 - (0 if early(n, p) else 1)

        block = ctx.enter_context(nc.Block())

        @block.sync
        def _(sp):
            st.load(sp, 0)
            w.load(sp, 0)
            st.load_gain(sp)
            w.load(sp, 1)
            with nc.allow_non_contiguous_dma(reason="per-channel constants, once"):
                for i in range(2):
                    cols = slice(i * P, (i + 1) * P)
                    sp.dma_start(taps[:, i, :], conv_dw[0, :, cols].rearrange("j p -> p j")).then_inc(small_loaded, 16)
                    for dst, src in ((conv_bias, conv_b), (ln_gain, conv_ln_g), (ln_bias, conv_ln_b)):
                        sp.dma_start(dst[:, i:i + 1], src[0, cols].rearrange("(p a) -> p a", a=1)).then_inc(small_loaded, 16)
            sp.dma_start(pw[:], conv_pw[0].rearrange("(i p) d -> p i d", p=P)).then_inc(small_loaded, 16)
            sp.dma_start(pscale.rearrange("p i d -> p (i d)"), pool_scale[0:1, :].to_broadcast([P, 2 * P])).then_inc(small_loaded, 16)
            sp.wait_ge(pool_w_zero, 1)
            for g in range(4):
                half = slice(g % 2 * 64, g % 2 * 64 + 64)
                sp.dma_start(pool_map[half, g // 2, half], pool_w[0, g]).then_inc(small_loaded, 16)
            for c in range(2, 5):
                w.load(sp, c)

            def store_pool(n):
                sp.wait_ge(y_pool_done, 2 * n + 2)
                sp.dma_start(y_scratch[Y_POOL:Y_POOL + 2, :, bass.ds(n * TB, TB)].rearrange("t p c -> p t c"),
                             y_pool[:]).then_inc(y_pool_stored, 16)

            def store_conv(n):
                sp.wait_ge(y_conv_done, 2 * n + 2)
                sp.dma_start(y_scratch[Y_CONV:Y_CONV + 2, :, bass.ds(n * TB, TB)].rearrange("t p c -> p t c"),
                             y_conv[:]).then_inc(y_conv_stored, 16)

            st.load(sp, 1)
            store_pool(0)
            with sp.Fori(1, NB - 1) as n:
                st.load(sp, n + 1)
                store_conv(n - 1)
                store_pool(n)
            store_conv(NB - 2)
            store_pool(NB - 1)
            store_conv(NB - 1)
            sp.wait_ge(y_pool_stored, 16 * NB)
            sp.wait_ge(y_conv_stored, 16 * NB)

        SMALL = 16 * (2 * 4 + 1 + 1 + 4)

        @block.gpsimd
        def _(pool):
            carrier = pool_carrier
            carrier.prepare(pool)
            nc.gpsimd.memset(pool_map[:], 0.0).then_inc(pool_w_zero, 1)
            for i in range(2):
                nc.gpsimd.iota(count[:, i, :], pattern=[[1, HALO]], base=1, channel_multiplier=0,
                               allow_small_or_imprecise_dtypes=True).then_inc(count_step, 1)
            st.prepare(pool, carrier)
            st.scale(pool, 0)

            def window_sums(n):
                pool.wait_ge(proj_free[0], earlier(n, SLOT["u0"]) + 1)
                pool.wait_ge(proj_free[1], earlier(n, SLOT["u1"]) + 1)
                step = 4 * n
                for i in range(2):
                    cur, width = u[:, i, :], 1
                    for level in range(2 * (i + 1)):
                        dst = sums[:, i, level % 2, :]
                        add = nc.gpsimd.tensor_tensor(dst[:, 2 * width:], cur[:, 2 * width:], cur[:, width:HALO + TB - width],
                                                      ALU.add)
                        cur, width = dst, 2 * width
                        if level < 2 * i + 1:
                            add.then_inc(pool_step, 1)
                            step += 1
                            pool.wait_ge(pool_step, step)
                    add.then_inc(sums_done, 1)

            def window_diffs(n):
                for i in range(2):
                    pool.wait_ge(means_done, 2 * n + i + 1)
                    if isinstance(n, int) and n == 0:
                        nc.gpsimd.tensor_tensor(diff[:, i, 0:HALO], diff[:, i, 0:HALO], widen[:, i, :],
                                                ALU.mult).then_inc(widen_ready, 1)
                        pool.wait_ge(widen_ready, 2 + i)
                    nc.gpsimd.tensor_tensor(diff[:, i, :], diff[:, i, :], u[:, i, HALO:], ALU.subtract).then_inc(diff_done, 1)

            def layer_norm_rstd(n):
                carrier.pool_wait(pool, meanvar_done, SUB * n + SUB)
                nc.gpsimd.tensor_scalar(var_eps[:], meanvar[:, :, 1], EPS, 1.0, ALU.add, ALU.mult).then_inc(rstd_step, 1)
                nc.gpsimd.tensor_scalar(neg_mean[:], meanvar[:, :, 0], -1.0, 1.0, ALU.mult, ALU.mult).then_inc(rstd_step, 1)
                pool.wait_ge(rstd_step, 4 * n + 2)
                nc.gpsimd.tensor_tensor(ln_rstd[:], var_eps[:], st.neg_half[:], ALU.pow).then_inc(rstd_step, 1)
                pool.wait_ge(rstd_step, 4 * n + 3)
                nc.gpsimd.tensor_tensor(ln_shift[:], neg_mean[:], ln_rstd[:], ALU.mult).then_inc(rstd_step, 1)

            def gate_conv(n, at):
                for i in range(2):
                    pool.wait_ge(proj_free[i], earlier(at[0], at[1] + i) + 1)
                    nc.gpsimd.tensor_tensor(y_conv[:, i, :], y_conv[:, i, :], gate_c[:, i, :], ALU.mult).then_inc(y_conv_done, 1)

            def gate_pool(n):
                for i in range(2):
                    pool.wait_ge(proj_free[i], earlier(n, SLOT[f"po{i}"]) + 1)
                    nc.gpsimd.tensor_tensor(y_pool[:, i, :], y_pool[:, i, :], gate_p[:, i, :], ALU.mult).then_inc(y_pool_done, 1)

            def body(n, more):
                if isinstance(n, int) and n == 0:
                    pool.wait_ge(widen_ready, 1)
                else:
                    layer_norm_rstd(n - 1)
                if more:
                    st.scale(pool, n + 1)
                window_sums(n)
                if not isinstance(n, int) or n > 0:
                    gate_conv(n - 1, (n, SLOT["pw0"]))
                window_diffs(n)
                gate_pool(n)

            body(0, True)
            with pool.Fori(1, NB - 1) as n:
                body(n, True)
            body(NB - 1, False)
            layer_norm_rstd(NB - 1)
            gate_conv(NB - 1, (NB, 0))

        @block.scalar
        def _(act):
            st.square(act, 0)
            for c in range(5):
                w.split_hi(act, c)
            act.wait_ge(small_loaded, SMALL)

            def from_proj(n, name, out, func, scale=1.0):
                p = SLOT[name]
                act.wait_ge(proj_full, filled(n, p))
                nc.scalar.activation(out, proj[p % 2][:], func, scale=scale).then_inc(proj_free[p % 2], 1)

            def layer_norm_apply(n):
                act.wait_ge(rstd_step, 4 * n + 4)
                for s in range(SUB):
                    nc.scalar.activation(z[:, s, :], tok[s // 2][:, s % 2, :], ACT.Identity, scale=ln_rstd[:, s:s + 1],
                                         bias=ln_shift[:, s:s + 1]).then_inc(z_done, 1)

            def norm_silu(n):
                for i in range(2):
                    act.wait_ge(z_turned, 2 * n + i + 1)
                    nc.scalar.activation(hs[:, i, :], feat[i][:], ACT.Silu, scale=ln_gain[:, i:i + 1],
                                         bias=ln_bias[:, i:i + 1]).then_inc(hs_done, 1)

            def copy_conv(n, at):
                need(act, y_conv_stored, 16 * n)
                for i in range(2):
                    p = at[1] + i
                    act.wait_ge(proj_full, filled(at[0], p))
                    nc.scalar.activation(y_conv[:, i, :], proj[p % 2][:], ACT.Copy).then_inc(proj_free[p % 2], 1)

            def window_means(n):
                for i in range(2):
                    act.wait_ge(sums_done, 2 * n + i + 1)
                    for g in (2 * i, 2 * i + 1):
                        half = slice(g % 2 * 64, g % 2 * 64 + 64)
                        last = nc.scalar.activation(diff[half, i, :], sums[half, i, g % 2, HALO:], ACT.Copy,
                                                    scale=1.0 / POOL_WINDOWS[g])
                    last.then_inc(means_done, 1)

            def body(n, more):
                first = isinstance(n, int) and n == 0
                for kk in range(KT):
                    st.split_hi(act, n, kk)
                from_proj(n, "cb0", sig[:, 0, :], ACT.Tanh, 0.5)
                if not first:
                    layer_norm_apply(n - 1)
                from_proj(n, "cb1", sig[:, 1, :], ACT.Tanh, 0.5)
                if more:
                    st.square(act, n + 1)
                if not first:
                    norm_silu(n - 1)
                act.wait_ge(proj_full, filled(n, SLOT["u0"]))
                if first:
                    act.wait_ge(halo_zero, 2)
                else:
                    act.wait_ge(diff_done, 2 * n)
                    nc.scalar.activation(u[:, :, 0:HALO], u[:, :, TB:], ACT.Copy).then_inc(u_halo, 1)
                    act.wait_ge(u_halo, n)
                for i in range(2):
                    from_proj(n, f"u{i}", u[:, i, HALO:], ACT.Copy)
                if not first:
                    copy_conv(n - 1, (n, SLOT["pw0"]))
                    act.wait_ge(y_pool_done, 2 * n)
                from_proj(n, "gp0", gate_p[:, 0, :], ACT.Silu)
                window_means(n)
                from_proj(n, "gp1", gate_p[:, 1, :], ACT.Silu)
                if not first:
                    act.wait_ge(y_conv_done, 2 * n)
                for i in range(2):
                    from_proj(n, f"gc{i}", gate_c[:, i, :], ACT.Silu)
                need(act, y_pool_stored, 16 * n)
                for i in range(2):
                    p = SLOT[f"po{i}"]
                    act.wait_ge(proj_full, filled(n, p))
                    nc.scalar.activation(y_pool[:, i, :], proj[p % 2][:], ACT.Copy).then_inc(proj_free[p % 2], 1)

            body(0, True)
            with act.Fori(1, NB - 1) as n:
                body(n, True)
            body(NB - 1, False)
            layer_norm_apply(NB - 1)
            norm_silu(NB - 1)
            copy_conv(NB - 1, (NB, 0))

        @block.vector
        def _(dve):
            carrier = dve_carrier
            carrier.prepare(dve)
            nc.vector.memset(h[:, :, 0:PAD], 0.0).then_inc(halo_zero, 1)
            nc.vector.memset(u[:, :, 0:HALO], 0.0).then_inc(halo_zero, 1)
            for c in range(5):
                w.split_lo(dve, c)
            dve.wait_ge(small_loaded, SMALL)
            nc.vector.tensor_scalar(taps[:], taps[:], 0.5, None, ALU.mult).then_inc(taps_ready, 1)
            nc.vector.tensor_tensor(pool_lhs[:], pool_map[:], pscale[:], ALU.mult).then_inc(pool_lhs_ready, 1)
            dve.wait_ge(count_step, 2)
            for g, window in enumerate(POOL_WINDOWS):
                half = slice(g % 2 * 64, g % 2 * 64 + 64)
                nc.vector.tensor_scalar(count[half, g // 2, :], count[half, g // 2, :], 1.0 / window, 1.0, ALU.mult,
                                        ALU.min).then_inc(count_step, 1)
            dve.wait_ge(count_step, 6)
            nc.vector.reciprocal(widen[:], count[:]).then_inc(widen_ready, 1)
            dve.wait_ge(taps_ready, 1)
            dve.wait_ge(halo_zero, 2)

            def glu(n, i):
                p = SLOT[f"ca{i}"]
                if not (isinstance(n, int) and n == 0):
                    dve.wait_ge(tap_done[i], TAPS * n)
                    nc.vector.tensor_copy(h[:, i, 0:PAD], h[:, i, TB:]).then_inc(h_halo[i], 1)
                    dve.wait_ge(h_halo[i], n)
                b = SLOT[f"cb{i}"]
                dve.wait_ge(proj_free[b % 2], earlier(n, b) + 1)
                dve.wait_ge(proj_full, filled(n, p))
                nc.vector.scalar_tensor_tensor(out=h[:, i, PAD:], in0=sig[:, i, :], scalar=1.0, in1=proj[p % 2][:],
                                               op0=ALU.add, op1=ALU.mult).then_inc(proj_free[p % 2], 1)

            def tap(n, i, j):
                if j == 0:
                    p = SLOT[f"ca{i}"]
                    dve.wait_ge(proj_free[p % 2], earlier(n, p) + 1)
                    need(dve, conv_turned, 2 * n)
                    nc.vector.tensor_scalar(conv[:, i, :], h[:, i, 0:TB], taps[:, i, 0:1], conv_bias[:, i:i + 1],
                                            ALU.mult, ALU.add).then_inc(tap_done[i], 1)
                else:
                    dve.wait_ge(tap_done[i], TAPS * n + j)
                    nc.vector.scalar_tensor_tensor(out=conv[:, i, :], in0=h[:, i, j:j + TB], scalar=taps[:, i, j:j + 1],
                                                   in1=conv[:, i, :], op0=ALU.mult, op1=ALU.add).then_inc(tap_done[i], 1)

            def layer_norm_stats(n):
                for s in range(SUB):
                    dve.wait_ge(conv_turned, 2 * n + s // 2 + 1)
                    nc.vector.bn_stats(stats[:, s, :], tok[s // 2][:, s % 2, :]).then_inc(stats_done, 1)
                carrier.dve_wait(dve, stats_done, SUB * n + SUB)
                for s in range(SUB):
                    nc.vector.bn_aggr(meanvar[:, s, :], stats[:, s, :]).then_inc(meanvar_done, 1)

            LEAD, LEFT, BESIDE_LO = 12, 10, 4
            ORDER = [(0, j) for j in range(LEAD)]
            for j in range(LEAD, TAPS):
                ORDER += [(0, j), (1, j - LEAD)]
            ORDER += [(1, j) for j in range(TAPS - LEAD, TAPS)]
            RUN = len(ORDER) - LEFT

            def some_taps(n, lo, hi):
                for i, j in ORDER[lo:hi]:
                    tap(n, i, j)

            def body(n):
                first = isinstance(n, int) and n == 0
                for kk in range(KT):
                    st.split_lo(dve, n, kk)
                    if not first and kk < BESIDE_LO:
                        some_taps(n - 1, RUN + kk, RUN + kk + 1)
                if not first:
                    some_taps(n - 1, RUN + BESIDE_LO, len(ORDER))
                glu(n, 0)
                if not first:
                    layer_norm_stats(n - 1)
                some_taps(n, 0, LEAD)
                glu(n, 1)
                some_taps(n, LEAD, RUN)

            body(0)
            with dve.Fori(1, NB) as n:
                body(n)
            some_taps(NB - 1, RUN, len(ORDER))
            layer_norm_stats(NB - 1)

        @block.tensor
        def _(pe):
            def project(n, name, between=None):
                p, c = SLOT[name], CHUNK_OF[name[:-1]]
                cols = slice(int(name[-1]) * P, int(name[-1]) * P + P)
                need(pe, proj_free[p % 2], earlier(n, p))
                if isinstance(n, int) and n == 0:
                    pe.wait_ge(w.lo_done, c + 1)
                for kk in range(KT):
                    if name == "cb0":
                        pe.wait_ge(st.lo_done, KT * n + kk + 1)
                    last = split3(nc, proj[p % 2][:], w.hi[:, c, kk, cols], w.lo[:, c, kk, cols], st.hi[:, kk, :],
                                  st.lo[:, kk, :], kk == 0, kk == KT - 1)
                    if between:
                        between(kk)
                last.then_inc(proj_full, 1)

            def turn_conv(n):
                for i in range(2):
                    pe.wait_ge(tap_done[i], TAPS * n + TAPS)
                for b in range(2):
                    for s in (2 * b, 2 * b + 1):
                        for i in range(2):
                            last = nc.tensor.transpose(tok[b][:, s % 2, i * P:(i + 1) * P],
                                                       conv[:, i, s * P:(s + 1) * P], st.ident[:])
                    last.then_inc(conv_turned, 1)

            def turn_z(n):
                pe.wait_ge(z_done, SUB * n + SUB)
                for i in range(2):
                    for s in range(SUB):
                        last = nc.tensor.transpose(feat[i][:, s * P:(s + 1) * P], z[:, s, i * P:(i + 1) * P], st.ident[:])
                    last.then_inc(z_turned, 1)

            def pointwise(n, at):
                pe.wait_ge(hs_done, 2 * n + 2)
                for o in range(2):
                    p = at[1] + o
                    need(pe, proj_free[p % 2], earlier(at[0], p))
                    for i in range(2):
                        last = nc.tensor.matmul(proj[p % 2][:], pw[:, i, o * P:(o + 1) * P], hs[:, i, :],
                                                start=(i == 0), stop=(i == 1))
                    last.then_inc(proj_full, 1)

            def map_pool(n):
                pe.wait_ge(diff_done, 2 * n + 2)
                if isinstance(n, int) and n == 0:
                    pe.wait_ge(pool_lhs_ready, 1)
                for i in range(2):
                    p = SLOT[f"po{i}"]
                    need(pe, proj_free[p % 2], earlier(n, p))
                    nc.tensor.matmul(proj[p % 2][:], pool_lhs[:, i, :], diff[:, i, :], start=True, stop=True).then_inc(proj_full, 1)

            def body(n):
                first = isinstance(n, int) and n == 0
                for kk in range(TURNS):
                    st.transpose(pe, n, kk)
                project(n, "cb0", lambda kk: st.transpose(pe, n, kk + TURNS) if kk + TURNS < KT else None)
                project(n, "ca0")
                if not first:
                    turn_conv(n - 1)
                project(n, "cb1")
                project(n, "ca1")
                if not first:
                    turn_z(n - 1)
                project(n, "u0")
                project(n, "u1")
                if first:
                    pe.wait_ge(small_loaded, SMALL)
                else:
                    pointwise(n - 1, (n, SLOT["pw0"]))
                for name in ("gp0", "gp1", "gc0", "gc1"):
                    project(n, name)
                map_pool(n)

            body(0)
            with pe.Fori(1, NB) as n:
                body(n)
            turn_conv(NB - 1)
            turn_z(NB - 1)
            pointwise(NB - 1, (NB, 0))


def output_phase(nc, x, w_out, final_g, y_scratch, out):
    ctx = ExitStack()
    with ctx:
        sb = lambda name, shape, dt=F32: ctx.enter_context(nc.sbuf_tensor("o_" + name, shape, dt))
        sem = lambda name: ctx.enter_context(nc.semaphore("o_" + name))
        pool_carrier = Carrier(nc, ctx, "o_pool_carrier")
        w_hi = sb("w_hi", [P, KT, D], F32R)
        w_lo = sb("w_lo", [P, KT, D], F32R)
        stage = sb("stage", [P, 2, D])
        y = sb("y", [P, KT, TB])
        y_hi = sb("y_hi", [P, 2, KT, TB], F32R)
        y_lo = sb("y_lo", [P, 2, KT, TB], F32R)
        xs = sb("xs", [P, 2, SUB, D])
        squares = sb("squares", [P, D])
        res = sb("res", [P, 2, D])
        gain = sb("gain", [P, D])
        sumsq = sb("sumsq", [P, 2, SUB])
        meansq = sb("meansq", [P, 2, SUB])
        rstd = sb("rstd", [P, 2, SUB])
        neg_half = sb("neg_half", [P, 1])
        acc = [ctx.enter_context(nc.psum_tensor(f"o_acc{b}", [P, TB], F32)) for b in range(4)]

        w_loaded = [sem("w_loaded0"), sem("w_loaded1")]
        w_hi_done = sem("w_hi_done")
        w_lo_done = sem("w_lo_done")
        gain_loaded = sem("gain_loaded")
        half_ready = sem("half_ready")
        x_loaded = [sem("x_loaded0"), sem("x_loaded1")]
        y_loaded = sem("y_loaded")
        y_hi_done = sem("y_hi_done")
        y_lo_done = sem("y_lo_done")
        acc_full = sem("acc_full")
        added = sem("added")
        squared = sem("squared")
        rstd_step = sem("rstd_step")
        finished = sem("finished")
        stored = [sem("stored0"), sem("stored1")]

        block = ctx.enter_context(nc.Block())

        @block.sync
        def _(sp):
            def load_x(n, b):
                need(sp, finished, SUB * (n - 1))
                sp.dma_start(xs[:, b], x[0, bass.ds(n * TB, TB), :].rearrange("(s p) d -> p s d", p=P)).then_inc(x_loaded[b], 16)

            def load_w(k):
                need(sp, w_lo_done, k - 1)
                dst = stage[:, k % 2, :]
                if k < Y_ATTN:
                    sp.dma_start(dst, w_out[0, k * P:(k + 1) * P, :]).then_inc(w_loaded[k % 2], 16)
                else:
                    for half in range(2):
                        row = POOL_W + CONV_W + (half * GROUP + k - Y_ATTN) * HD
                        sp.dma_start(dst[half * HD:(half + 1) * HD], w_out[0, row:row + HD, :]).then_inc(w_loaded[k % 2], 16)

            def store(n, s):
                sp.wait_ge(finished, SUB * n + s + 1)
                sp.dma_start(out[0, bass.ds(n * TB + s * P, P), :], res[:, s % 2, :]).then_inc(stored[s % 2], 16)

            for k in range(KT):
                load_w(k)
            sp.dma_start(gain[:], final_g.rearrange("(a d) -> a d", a=1).to_broadcast([P, D])).then_inc(gain_loaded, 16)
            load_x(0, 0)
            load_x(1, 1)

            def body(n, b, more):
                for s in range(SUB):
                    store(n, s)
                if more:
                    load_x(n + 2, b)

            with sp.Fori(0, NB // 2 - 1) as pair:
                body(2 * pair, 0, True)
                body(2 * pair + 1, 1, True)
            body(NB - 2, 0, False)
            body(NB - 1, 1, False)
            for b in range(2):
                sp.wait_ge(stored[b], 16 * 2 * NB)

        @block.gpsimd
        def _(pool):
            carrier = pool_carrier
            carrier.prepare(pool)
            nc.gpsimd.memset(neg_half[:], -0.5).then_inc(half_ready, 1)
            pool.wait_ge(half_ready, 1)

            def body(n, b):
                for s in range(SUB):
                    col = slice(s, s + 1)
                    carrier.pool_wait(pool, squared, SUB * n + s + 1)
                    nc.gpsimd.tensor_scalar(meansq[:, b, col], sumsq[:, b, col], 1.0 / D, EPS, ALU.mult,
                                            ALU.add).then_inc(rstd_step, 1)
                    pool.wait_ge(rstd_step, 2 * SUB * n + 2 * s + 1)
                    nc.gpsimd.tensor_tensor(rstd[:, b, col], meansq[:, b, col], neg_half[:], ALU.pow).then_inc(rstd_step, 1)

            with pool.Fori(0, NB, 2) as n:
                body(n, 0)
                body(n + 1, 1)

        @block.scalar
        def _(act):
            def load_y(n):
                need(act, y_lo_done, KT * n)
                act.dma_start(y[:], y_scratch[:, :, bass.ds(n * TB, TB)].rearrange("t p c -> p t c")).then_inc(y_loaded, 16)

            load_y(0)

            def split(n, b, k):
                act.wait_ge(y_loaded, 16 * n + 16)
                if k == 0:
                    need(act, acc_full, 8 * n - 8)
                nc.scalar.activation(y_hi[:, b, k, :], y[:, k, :], ACT.Copy).then_inc(y_hi_done, 1)

            for k in range(KT):
                split(0, 0, k)
                act.wait_ge(w_loaded[k % 2], 16 * (k // 2 + 1) if k < Y_ATTN else 16 * (2 + 2 * ((k - Y_ATTN) // 2 + 1)))
                nc.scalar.activation(w_hi[:, k, :], stage[:, k % 2, :], ACT.Copy).then_inc(w_hi_done, 1)

            def body(n, b, more):
                for s in range(SUB):
                    if more:
                        split(n + 1, 1 - b, 2 * s)
                        split(n + 1, 1 - b, 2 * s + 1)
                    act.wait_ge(added, 8 * n + 2 * s + 2)
                    if not isinstance(n, int) or n > 0 or s > 0:
                        act.wait_ge(squared, SUB * n + s)
                    nc.scalar.activation(squares[:], xs[:, b, s, :], ACT.Square,
                                         accum_out=sumsq[:, b, s:s + 1]).then_inc(squared, 1)
                if more > 1:
                    load_y(n + 2)

            load_y(1)
            body(0, 0, NB - 1)
            with act.Fori(1, NB - 3, 2) as n:
                body(n, 1, 2)
                body(n + 1, 0, 2)
            body(NB - 3, 1, 2)
            body(NB - 2, 0, 1)
            body(NB - 1, 1, 0)

        @block.vector
        def _(dve):
            def split(n, b, k):
                dve.wait_ge(y_hi_done, KT * n + k + 1)
                nc.vector.tensor_tensor(y_lo[:, b, k, :], y[:, k, :], y_hi[:, b, k, :].bitcast(F32),
                                        ALU.subtract).then_inc(y_lo_done, 1)

            for k in range(KT):
                split(0, 0, k)
                dve.wait_ge(w_hi_done, k + 1)
                nc.vector.tensor_tensor(w_lo[:, k, :], stage[:, k % 2, :], w_hi[:, k, :].bitcast(F32),
                                        ALU.subtract).then_inc(w_lo_done, 1)
            dve.wait_ge(gain_loaded, 16)

            def finish(n, b, s):
                dve.wait_ge(rstd_step, 2 * SUB * n + 2 * s + 2)
                if not isinstance(n, int) or n > 0 or s >= 2:
                    dve.wait_ge(stored[s % 2], 16 * 2 * n + 16 * (s // 2))
                nc.vector.scalar_tensor_tensor(out=res[:, s % 2, :], in0=xs[:, b, s, :], scalar=rstd[:, b, s:s + 1],
                                               in1=gain[:], op0=ALU.mult, op1=ALU.mult).then_inc(finished, 1)

            def body(n, b, more, uses):
                dve.wait_ge(x_loaded[b], uses)
                for s in range(SUB):
                    if more:
                        split(n + 1, 1 - b, 2 * s)
                        split(n + 1, 1 - b, 2 * s + 1)
                    for half in range(2):
                        cols = slice(half * TB, (half + 1) * TB)
                        dve.wait_ge(acc_full, 8 * n + 2 * s + half + 1)
                        nc.vector.tensor_tensor(xs[:, b, s, cols], acc[s % 2 * 2 + half][:], xs[:, b, s, cols],
                                                ALU.add).then_inc(added, 1)
                    if s:
                        finish(n, b, s - 1)
                finish(n, b, SUB - 1)

            body(0, 0, True, 16)
            with dve.Fori(1, NB - 1, 2) as n:
                body(n, 1, True, 8 * n + 8)
                body(n + 1, 0, True, 8 * n + 24)
            body(NB - 1, 1, False, 8 * NB)

        @block.tensor
        def _(pe):
            def body(n, b):
                for s in range(SUB):
                    toks = slice(s * P, (s + 1) * P)
                    for half in range(2):
                        cols = slice(half * TB, (half + 1) * TB)
                        bank = s % 2 * 2 + half
                        if not isinstance(n, int) or n > 0 or s >= 2:
                            pe.wait_ge(added, 8 * n + 2 * s + half - 3)
                        for k in range(KT):
                            if s == 0 and half == 0:
                                pe.wait_ge(y_lo_done, KT * n + k + 1)
                                if isinstance(n, int) and n == 0:
                                    pe.wait_ge(w_lo_done, k + 1)
                            last = split3(nc, acc[bank][:], y_hi[:, b, k, toks], y_lo[:, b, k, toks],
                                          w_hi[:, k, cols], w_lo[:, k, cols], k == 0, k == KT - 1)
                        last.then_inc(acc_full, 1)

            body(0, 0)
            with pe.Fori(1, NB - 1, 2) as n:
                body(n, 1)
                body(n + 1, 0)
            body(NB - 1, 1)


def build(nc, x, ln_g, w_in, pool_w, pool_scale, conv_dw, conv_b, conv_ln_g, conv_ln_b, conv_pw, attn_sinks,
          w_out, final_g, out):
    y_scratch = nc.dram_tensor("y_scratch", (KT, P, S), F32, kind="Internal").ap()
    attention_phase(nc, x, ln_g, w_in, attn_sinks, y_scratch)
    mixer_phase(nc, x, ln_g, w_in, pool_w, pool_scale, conv_dw, conv_b, conv_ln_g, conv_ln_b, conv_pw, y_scratch)
    output_phase(nc, x, w_out, final_g, y_scratch, out)


_INS = ["x", "ln_g", "w_in", "pool_w", "pool_scale", "conv_dw", "conv_b", "conv_ln_g", "conv_ln_b", "conv_pw",
        "attn_sinks", "w_out", "final_g"]


def kernel(**inputs):
    import numpy as _np
    import concourse.bacc as _bacc
    from concourse import mybir as _mybir
    from concourse.bass_utils import run_bass_kernel_spmd as _run

    nc = _bacc.Bacc("TRN2", target_bir_lowering=False, num_devices=1)
    arrays, args = {}, []
    for name in _INS:
        a = _np.ascontiguousarray(inputs[name])
        arrays[f"in_{name}_dram"] = a
        args.append(nc.dram_tensor(f"in_{name}_dram", a.shape, _mybir.dt.from_np(a.dtype), kind="ExternalInput").ap())
    out = nc.dram_tensor("out_dram", (1, S, D), _mybir.dt.float32, kind="ExternalOutput").ap()
    build(nc, *args, out)
    r = _run(nc, [arrays], core_ids=[0])
    return r.results[0]["out_dram"]
```

```python
from contextlib import ExitStack

import concourse.bass as bass
from concourse import mybir

F32 = mybir.dt.float32
F32R = mybir.dt.float32r
ALU = mybir.AluOpType
ACT = mybir.ActivationFunctionType

P = 128
D = 1024
S = 4096
KT = D // P
TB = 512
NB = S // TB
SUB = TB // P
POOL_W = 256
CONV_W = 256
TAPS = 31
HEADS = 8
KV = 2
GROUP = HEADS // KV
HD = 64
ATTN_W = HEADS * HD
WINDOW = 128
EPS = 1e-6
MASKED = -1e30
CHUNK = 256
SLOTS = 5
POOL_WINDOWS = (2, 4, 8, 16)
HALO = 16
TURNS = 4
PAD = TAPS - 1

COL_U = 0
COL_GP = COL_U + POOL_W
COL_CA = COL_GP + POOL_W
COL_CB = COL_CA + CONV_W
COL_GC = COL_CB + CONV_W
COL_Q = COL_GC + CONV_W
COL_K = COL_Q + ATTN_W
COL_V = COL_K + KV * HD
COL_GA = COL_V + KV * HD

Y_POOL, Y_CONV, Y_ATTN = 0, 2, 4


def need(engine, sem, count):
    if not isinstance(count, int) or count > 0:
        engine.wait_ge(sem, count)


class Carrier:

    CELLS = 8

    def __init__(self, nc, ctx, name):
        self.nc = nc
        self.cell = ctx.enter_context(nc.sbuf_tensor(name, [P, 1 + self.CELLS], F32))
        self.uses = 0
        self.ready = ctx.enter_context(nc.semaphore(name + "_ready"))

    def prepare(self, engine):
        engine.memset(self.cell[:], 0.0).then_inc(self.ready, 1)
        engine.wait_ge(self.ready, 1)

    def next_cell(self):
        self.uses += 1
        return self.cell[:, 1 + self.uses % self.CELLS:2 + self.uses % self.CELLS]

    def dve_wait(self, dve, sem, count):
        dve.wait_ge(sem, count)
        if not isinstance(count, int):
            self.nc.vector.tensor_copy(self.next_cell(), self.cell[:, 0:1])

    def pool_wait(self, pool, sem, count):
        pool.wait_ge(sem, count)
        if not isinstance(count, int):
            self.nc.gpsimd.tensor_tensor(self.next_cell(), self.cell[:, 0:1], self.cell[:, 0:1], ALU.add)


def identity(nc, pool, ident, sem):
    nc.gpsimd.memset(ident[:], 0.0).then_inc(sem, 1)
    pool.wait_ge(sem, 1)
    nc.gpsimd.affine_select(out=ident[:], in_=ident[:], compare_op=ALU.not_equal, fill=1.0,
                            base=0, pattern=[[-1, P]], channel_multiplier=1).then_inc(sem, 1)


class XStage:

    def __init__(self, nc, ctx, x, ln_g):
        self.nc, self.x, self.ln_g = nc, x, ln_g
        sb = lambda name, shape, dt=F32: ctx.enter_context(nc.sbuf_tensor(name, shape, dt))
        sem = lambda name: ctx.enter_context(nc.semaphore(name))
        self.xs = sb("xs", [P, SUB, D])
        self.sumsq = sb("sumsq", [P, SUB])
        self.meansq = sb("meansq", [P, SUB])
        self.rstd = sb("rstd", [P, SUB])
        self.neg_half = sb("neg_half", [P, SUB])
        self.gain = sb("gain", [P, KT])
        self.ident = sb("ident", [P, P])
        self.hi = sb("xT_hi", [P, KT, TB], F32R)
        self.lo = sb("xT_lo", [P, KT, TB], F32R)
        self.loaded = [sem(f"x_loaded{s}") for s in range(SUB)]
        self.gain_loaded = sem("gain_loaded")
        self.ident_ready = sem("ident_ready")
        self.half_ready = sem("half_ready")
        self.squared = sem("x_squared")
        self.rstd_steps = sem("rstd_steps")
        self.scaled = sem("x_scaled")
        self.turned = sem("x_turned")
        self.hi_done = sem("xT_hi_done")
        self.lo_done = sem("xT_lo_done")

    def use(self, base, turn, squares):
        self.base, self.turn, self.squares = base, turn, squares

    def load(self, sp, n, block=None):
        block = n if block is None else block
        need(sp, self.turned, KT * (self.base + n))
        for s in range(SUB):
            sp.dma_start(self.xs[:, s, :], self.x[0, bass.ds(block * TB + s * P, P), :]).then_inc(self.loaded[s], 16)

    def lo_count(self, n, k):
        return KT * (self.base + n) + k + 1

    def load_gain(self, sp):
        with self.nc.allow_non_contiguous_dma(reason="1024 values, once"):
            sp.dma_start(self.gain[:], self.ln_g[0].rearrange("(k p) -> p k", p=P)).then_inc(self.gain_loaded, 16)

    def square(self, act, n):
        n = self.base + n
        for s in range(SUB):
            act.wait_ge(self.loaded[s], 16 * n + 16)
            if not isinstance(n, int) or n > 0 or s > 0:
                act.wait_ge(self.squared, SUB * n + s)
            self.nc.scalar.activation(self.squares[:], self.xs[:, s, :], ACT.Square,
                                      accum_out=self.sumsq[:, s:s + 1]).then_inc(self.squared, 1)

    def prepare(self, pool):
        self.nc.gpsimd.memset(self.neg_half[:], -0.5).then_inc(self.half_ready, 1)
        identity(self.nc, pool, self.ident, self.ident_ready)
        pool.wait_ge(self.half_ready, 1)

    def scale(self, pool, n, carrier, rows=range(SUB)):
        nc, n = self.nc, self.base + n
        carrier.pool_wait(pool, self.squared, SUB * n + SUB)
        nc.gpsimd.tensor_scalar(self.meansq[:], self.sumsq[:], 1.0 / D, EPS, ALU.mult, ALU.add).then_inc(self.rstd_steps, 1)
        pool.wait_ge(self.rstd_steps, 2 * n + 1)
        nc.gpsimd.tensor_tensor(self.rstd[:], self.meansq[:], self.neg_half[:], ALU.pow).then_inc(self.rstd_steps, 1)
        carrier.pool_wait(pool, self.rstd_steps, 2 * n + 2)
        for s in rows:
            nc.gpsimd.tensor_scalar(self.xs[:, s, :], self.xs[:, s, :], self.rstd[:, s:s + 1], 1.0,
                                    ALU.mult, ALU.mult).then_inc(self.scaled, 1)

    def scale_rows(self, dve, n, rows):
        dve.wait_ge(self.rstd_steps, 2 * n + 2)
        for s in rows:
            self.nc.vector.tensor_scalar(self.xs[:, s, :], self.xs[:, s, :], self.rstd[:, s:s + 1], None,
                                         ALU.mult).then_inc(self.scaled, 1)

    def transpose(self, pe, n, k):
        n = self.base + n
        if k == 0:
            pe.wait_ge(self.scaled, SUB * n + SUB)
            if isinstance(n, int) and n == 0:
                pe.wait_ge(self.ident_ready, 2)
        if k >= TURNS:
            pe.wait_ge(self.lo_done, KT * n + k - TURNS + 1)
        for s in range(SUB):
            last = self.nc.tensor.transpose(self.turn[k % TURNS][:, s * P:(s + 1) * P],
                                            self.xs[:, s, k * P:(k + 1) * P], self.ident[:])
        last.then_inc(self.turned, 1)

    def split_hi(self, act, n, k):
        n = self.base + n
        if isinstance(n, int) and n == 0 and k == 0:
            act.wait_ge(self.gain_loaded, 16)
        act.wait_ge(self.turned, KT * n + k + 1)
        self.nc.scalar.activation(self.hi[:, k, :], self.turn[k % TURNS][:], ACT.Copy,
                                  scale=self.gain[:, k:k + 1]).then_inc(self.hi_done, 1)

    def split_lo(self, dve, n, k):
        n = self.base + n
        dve.wait_ge(self.hi_done, KT * n + k + 1)
        self.nc.vector.scalar_tensor_tensor(out=self.lo[:, k, :], in0=self.turn[k % TURNS][:],
                                            scalar=self.gain[:, k:k + 1], in1=self.hi[:, k, :].bitcast(F32),
                                            op0=ALU.mult, op1=ALU.subtract).then_inc(self.lo_done, 1)


def split3(nc, out, w_hi, w_lo, x_hi, x_lo, first, last):
    nc.tensor.matmul(out, w_hi, x_hi, start=first, stop=False)
    nc.tensor.matmul(out, w_lo, x_hi, start=False, stop=False)
    return nc.tensor.matmul(out, w_hi, x_lo, start=False, stop=last)


class Weights:

    def __init__(self, nc, ctx, w_in, w_out):
        self.nc = nc
        self.plan = [(w_in, col, CHUNK, slot) for col, slot in (
            (COL_K, 0), (COL_Q, 1), (COL_Q + CHUNK, 2), (COL_GA, 3), (COL_GA + CHUNK, 4),
            (COL_CB, 1), (COL_CA, 2), (COL_U, 0), (COL_GP, 3), (COL_GC, 4))]
        self.plan += [(w_out, half * TB, TB, half * TB // CHUNK) for half in range(2)]
        self.hi_buf = ctx.enter_context(nc.sbuf_tensor("w_hi", [P, SLOTS, KT * CHUNK], F32R))
        self.lo_buf = ctx.enter_context(nc.sbuf_tensor("w_lo", [P, SLOTS, KT * CHUNK], F32R))
        sem = lambda name: ctx.enter_context(nc.semaphore(name))
        self.loaded = [sem(f"w_loaded{c}") for c in range(len(self.plan))]
        self.hi_done = sem("w_hi_done")
        self.lo_done = [sem(f"w_lo_done{c}") for c in range(len(self.plan))]

    def chunk(self, buf, c):
        _, _, cols, slot = self.plan[c]
        return buf[:, slot:slot + cols // CHUNK].rearrange("p s c -> p (s c)").rearrange("p (k c) -> p k c", k=KT)

    def hi(self, c):
        return self.chunk(self.hi_buf, c)

    def lo(self, c):
        return self.chunk(self.lo_buf, c)

    def use(self, landing):
        flat = lambda a: a if len(a.shape) == 2 else a.rearrange("p a b -> p (a b)")
        self.landing = {c: flat(a).rearrange("p (k c) -> p k c", k=KT) for c, a in landing.items()}

    def load(self, sp, c):
        matrix, first, cols, _ = self.plan[c]
        sp.dma_start(self.landing[c], matrix[0, :, first:first + cols].rearrange("(k p) c -> p k c", p=P)
                     ).then_inc(self.loaded[c], 16)

    def split_hi(self, act, c):
        act.wait_ge(self.loaded[c], 16)
        self.nc.scalar.activation(self.hi(c), self.landing[c], ACT.Copy).then_inc(self.hi_done, 1)

    def split_lo_on_pool(self, pool, c):
        pool.wait_ge(self.hi_done, c + 1)
        self.nc.gpsimd.tensor_tensor(self.lo(c), self.landing[c], self.hi(c).bitcast(F32),
                                     ALU.subtract).then_inc(self.lo_done[c], 1)

    def split_lo(self, dve, c):
        dve.wait_ge(self.hi_done, c + 1)
        self.nc.vector.tensor_tensor(self.lo(c), self.landing[c], self.hi(c).bitcast(F32),
                                     ALU.subtract).then_inc(self.lo_done[c], 1)


CHUNK_K, CHUNK_Q, CHUNK_G = 0, 1, 3
CHUNK_CB, CHUNK_CA, CHUNK_U, CHUNK_GP, CHUNK_GC = 5, 6, 7, 8, 9
CHUNK_OUT = 10


def attention_phase(nc, st, w, y, y_stored, attn_sinks, y_scratch):
    ctx = ExitStack()
    with ctx:
        sb = lambda name, shape, dt=F32: ctx.enter_context(nc.sbuf_tensor("a_" + name, shape, dt))
        sem = lambda name: ctx.enter_context(nc.semaphore("a_" + name))
        pool_carrier = Carrier(nc, ctx, "a_pool_carrier")
        dve_carrier = Carrier(nc, ctx, "a_dve_carrier")
        bank = lambda name, shape: ctx.enter_context(nc.psum_tensor("a_" + name, shape, F32))
        proj = [bank(f"proj{b}", [P, TB]) for b in range(2)]
        score = bank("score", [P, HEADS, 2 * P])
        turn = [bank(f"turn{b}", [P, TB]) for b in range(2)]
        tanh = sb("tanh", [P, 2, TB])
        st.use(0, turn + [score[:, 2 * b:2 * b + 2].rearrange("p a b -> p (a b)") for b in (2, 3)], tanh.rearrange("p a b -> p (a b)"))
        rows = sb("rows", [P, 4, D])
        probs = rows[:, 0:2].rearrange("p b (h c) -> p b h c", h=HEADS)
        earlier_tile = rows[:, 2, 0:GROUP * P].rearrange("p (h c) -> p h c", h=GROUP)
        seen = rows[:, 3].rearrange("p (s c) -> p s c", s=2)

        q = sb("q", [P, HEADS, TB], F32R)
        k_hi = sb("k_hi", [P, KV, P + TB], F32R)
        k_lo = sb("k_lo", [P, P + TB], F32R)
        vT = tanh[:, 0]
        v = sb("v", [P, 1 + SUB, P])
        gate = sb("gate", [P, GROUP, TB])
        dist = gate[:, GROUP - 1, 0:2 * P]
        pT = sb("pT", [P, 2, KV, GROUP * P])
        bias = sb("bias", [P, 2, HEADS, P])
        w.use({CHUNK_K: rows[:, 0:2], CHUNK_Q: rows[:, 2:4], CHUNK_Q + 1: y, CHUNK_G: pT.rearrange("p a b c -> p (a b c)"),
               CHUNK_G + 1: rows[:, 0:2], CHUNK_CB: st.xs[:, 0:2], CHUNK_CA: st.xs[:, 2:4]})
        sinks = sb("sinks", [P, HEADS])
        rowmax = sb("rowmax", [P, 2, HEADS])
        negmax = sb("negmax", [P, 2, HEADS])
        sinkdiff = sb("sinkdiff", [P, 2, HEADS])
        sinkexp = sb("sinkexp", [P, 2, HEADS])
        rowsum = sb("rowsum", [P, 2, HEADS])
        denom = sb("denom", [P, 2, HEADS])
        inv = sb("inv", [P, 2, HEADS])

        halo_zero = sem("halo_zero")
        sinks_loaded = sem("sinks_loaded")
        bias_ready = sem("bias_ready")
        bias_step = sem("bias_step")
        proj_full = sem("proj_full")
        proj_free = [sem("proj_free0"), sem("proj_free1")]
        k_halo = sem("k_halo")
        k_lo_halo = sem("k_lo_halo")
        k_hi_done = sem("k_hi_done")
        q_hi_done = sem("q_hi_done")
        v_halo = sem("v_halo")
        v_turned = sem("v_turned")
        v_ready = sem("v_ready")
        score_full = sem("score_full")
        score_taken = sem("score_taken")
        row_step = sem("row_step")
        max_ready = sem("max_ready")
        exp_done = sem("exp_done")
        den_step = sem("den_step")
        probs_ready = sem("probs_ready")
        p_turned = sem("p_turned")
        pT_done = sem("pT_done")
        seen_ready = sem("seen_ready")
        take_step = sem("take_step")
        tanh_done = sem("tanh_done")
        gated = sem("gated")
        tail_gated = sem("tail_gated")

        SLOT = {name: p for p, name in enumerate(
            ["k", "q0", "o3", "q1", "q2", "q3", "v", "g0", "g1", "o0", "g2", "o1", "g3", "o2"])}
        USES = len(SLOT)

        def early(n, p):
            return isinstance(n, int) and n == 0 and p < SLOT["o3"]

        def filled(n, p):
            return USES * n + p + (1 if early(n, p) else 0)

        def earlier(n, p):
            return USES // 2 * n + p // 2 - (0 if p % 2 or early(n, p) else 1)

        def slot(name):
            return SLOT[name]

        halves = [slice(0, HD), slice(HD, P)]

        block = ctx.enter_context(nc.Block())

        @block.sync
        def _(sp):
            st.load(sp, 0)
            w.load(sp, CHUNK_K)
            st.load_gain(sp)
            sp.dma_start(sinks[:], attn_sinks[0:1, :].to_broadcast([P, HEADS])).then_inc(sinks_loaded, 16)
            for c in range(CHUNK_Q, CHUNK_CB):
                if c == CHUNK_G + 1:
                    sp.wait_ge(w.lo_done[CHUNK_K], 1)
                w.load(sp, c)

            def store(n):
                sp.wait_ge(gated, n + 1)
                sp.dma_start(y_scratch[Y_ATTN:Y_ATTN + GROUP, :, bass.ds(n * TB, TB)].rearrange("t p c -> p t c"),
                             y[:]).then_inc(y_stored, 16)

            st.load(sp, 1)
            with sp.Fori(1, NB - 1) as n:
                st.load(sp, n + 1)
                store(n - 1)
            sp.wait_ge(st.turned, KT * NB)
            w.load(sp, CHUNK_CB)
            w.load(sp, CHUNK_CA)
            store(NB - 2)
            sp.wait_ge(w.lo_done[CHUNK_CA], 1)
            st.load(sp, NB, 0)
            store(NB - 1)

        @block.gpsimd
        def _(pool):
            carrier = pool_carrier
            carrier.prepare(pool)
            nc.gpsimd.iota(dist[:], pattern=[[-1, 2 * P]], base=P, channel_multiplier=1,
                           allow_small_or_imprecise_dtypes=True).then_inc(bias_step, 1)
            st.prepare(pool)
            st.scale(pool, 0, carrier, range(2))
            pool.wait_ge(bias_step, 1)

            def alibi(tile, steps):
                lo = tile * P
                part = bias[:, tile]
                for h in range(HEADS):
                    last = nc.gpsimd.tensor_scalar(part[:, h], dist[:, lo:lo + P], -(2.0 ** (-8.0 * (h + 1) / HEADS)),
                                                   1.0, ALU.mult, ALU.mult)
                last.then_inc(bias_step, 1)
                pool.wait_ge(bias_step, steps + 1)
                nc.gpsimd.affine_select(out=part, in_=part, compare_op=ALU.is_ge, fill=MASKED, base=P - lo,
                                        pattern=[[0, HEADS], [-1, P]], channel_multiplier=1).then_inc(bias_step, 1)
                pool.wait_ge(bias_step, steps + 2)
                nc.gpsimd.affine_select(out=part, in_=part, compare_op=ALU.is_ge, fill=MASKED, base=WINDOW - 1 - P + lo,
                                        pattern=[[0, HEADS], [1, P]], channel_multiplier=-1).then_inc(bias_step, 1)

            alibi(1, 1)
            alibi(0, 4)
            def make_seen():
                pool.wait_ge(w.lo_done[CHUNK_Q], 1)
                nc.gpsimd.memset(seen, 1.0).then_inc(bias_step, 1)
                nc.gpsimd.memset(earlier_tile, 1.0).then_inc(bias_step, 1)
                pool.wait_ge(bias_step, 9)
                for tile in range(2):
                    part = seen[:, tile].rearrange("p (h c) -> p h c", h=GROUP)
                    sign = 1 if tile else -1
                    nc.gpsimd.affine_select(out=part, in_=part, compare_op=ALU.is_ge, fill=0.0, base=tile - 1,
                                            pattern=[[0, GROUP], [sign, P]], channel_multiplier=-sign).then_inc(seen_ready, 1)
                nc.gpsimd.affine_select(out=earlier_tile, in_=earlier_tile, compare_op=ALU.is_ge, fill=0.0, base=-1,
                                        pattern=[[0, GROUP], [1, P]], channel_multiplier=-1).then_inc(seen_ready, 1)

            def normalise(n, j):
                m, b = 4 * n + j, j % 2
                for kv in range(KV):
                    carrier.pool_wait(pool, den_step, 4 * m + 2 * kv + 2)
                    for t in range(GROUP):
                        h = kv * GROUP + t
                        last = nc.gpsimd.tensor_scalar(probs[:, b, h, :], probs[:, b, h, :], inv[:, b, h:h + 1], 0.5,
                                                       ALU.mult, ALU.mult)
                    last.then_inc(probs_ready, 1)

            def gate_output(n, at):
                pool.wait_ge(proj_free[at[1] % 2], earlier(*at) + 1)
                for t in range(GROUP):
                    last = nc.gpsimd.tensor_tensor(y[:, t, :], y[:, t, :], gate[:, t, :], ALU.mult)
                last.then_inc(gated, 1)

            def body(n):
                if not isinstance(n, int) or n > 0:
                    gate_output(n - 1, (n, slot("o3")))
                if not isinstance(n, int) or n < NB - 1:
                    st.scale(pool, n + 1, carrier)
                if isinstance(n, int) and n == 0:
                    make_seen()
                for j in range(SUB):
                    normalise(n, j)

            body(0)
            with pool.Fori(1, NB - 1) as n:
                body(n)
            body(NB - 1)
            st.scale(pool, NB, carrier)

        @block.scalar
        def _(act):
            st.square(act, 0)
            w.split_hi(act, CHUNK_K)

            def copy_out(n, p, out):
                act.wait_ge(proj_full, filled(n, p))
                nc.scalar.activation(out, proj[p % 2][:], ACT.Copy).then_inc(proj_free[p % 2], 1)

            def q_hi(n, t):
                p = slot(f"q{t}")
                act.wait_ge(proj_full, filled(n, p))
                for odd in range(2):
                    head = 2 * t + odd
                    last = nc.scalar.activation(q[halves[head // GROUP], head, :], proj[p % 2][halves[odd], :], ACT.Copy,
                                                scale=HD ** -0.5)
                    last.then_inc(q_hi_done, 1)

            def exps(n, j, kv):
                m, b = 4 * n + j, j % 2
                heads = slice(kv * GROUP, (kv + 1) * GROUP)
                act.wait_ge(max_ready, 2 * m + kv + 1)
                nc.scalar.activation(sinkexp[:, b, heads], sinkdiff[:, b, heads], ACT.Exp)
                for t in range(GROUP):
                    h = kv * GROUP + t
                    last = nc.scalar.activation(probs[:, b, h, :], probs[:, b, h, :], ACT.Exp,
                                                bias=negmax[:, b, h:h + 1], accum_out=rowsum[:, b, h:h + 1])
                last.then_inc(exp_done, 1)

            def gate_tanh(n, t):
                p = slot(f"g{t}")
                act.wait_ge(proj_full, filled(n, p))
                nc.scalar.activation(tanh[:, t % 2, :], proj[p % 2][:], ACT.Tanh, scale=0.5).then_inc(tanh_done, 1)

            def body(n):
                first, final = isinstance(n, int) and n == 0, isinstance(n, int) and n == NB - 1
                for kk in range(KT):
                    st.split_hi(act, n, kk)
                    if first and kk == 3:
                        w.split_hi(act, CHUNK_Q)
                act.wait_ge(proj_full, filled(n, slot("k")))
                if first:
                    act.wait_ge(halo_zero, 3)
                else:
                    nc.scalar.activation(k_hi[:, :, 0:P], k_hi[:, :, TB:TB + P], ACT.Copy).then_inc(k_halo, 1)
                    act.wait_ge(k_halo, n)
                for kv in range(KV):
                    for rows in halves:
                        last = nc.scalar.activation(k_hi[rows, kv, P:], proj[slot("k") % 2][halves[kv], :], ACT.Copy)
                last.then_inc(k_hi_done, 1)
                q_hi(n, 0)
                if first:
                    w.split_hi(act, CHUNK_Q + 1)
                q_hi(n, 1)
                if first:
                    w.split_hi(act, CHUNK_G)
                if not final:
                    st.square(act, n + 1)
                q_hi(n, 2)
                if first:
                    w.split_hi(act, CHUNK_G + 1)
                if final:
                    w.split_hi(act, CHUNK_CB)
                q_hi(n, 3)
                if final:
                    w.split_hi(act, CHUNK_CA)
                act.wait_ge(st.squared, SUB * NB if final else SUB * (n + 2))
                copy_out(n, slot("v"), vT)
                act.wait_ge(v_turned, n + 1)
                if not first:
                    nc.scalar.activation(v[:, 0, :], v[:, SUB, :], ACT.Copy).then_inc(v_halo, 1)
                    act.wait_ge(v_halo, n)
                nc.scalar.activation(v[:, 1:, :].rearrange("p a d -> p (a d)"), turn[1][:], ACT.Copy).then_inc(v_ready, 1)
                for j in range(SUB):
                    exps(n, j, 0)
                    if j:
                        gate_tanh(n, j)
                    exps(n, j, 1)
                    if j == 0:
                        gate_tanh(n, j)

            body(0)
            with act.Fori(1, NB - 1) as n:
                body(n)
            body(NB - 1)
            act.wait_ge(proj_free[slot("g3") % 2], earlier(NB - 1, slot("g3")) + 1)
            st.square(act, NB)

        @block.vector
        def _(dve):
            carrier = dve_carrier
            carrier.prepare(dve)
            for part in (k_hi[:, :, 0:P], k_lo[:, 0:P]):
                nc.vector.memset(part.bitcast(F32), 0.0).then_inc(halo_zero, 1)
            nc.vector.memset(v[:, 0, :], 0.0).then_inc(halo_zero, 1)
            st.scale_rows(dve, 0, range(2, SUB))
            w.split_lo(dve, CHUNK_K)
            dve.wait_ge(sinks_loaded, 16)

            def take_scores(n, j, kv):
                m, b = 4 * n + j, j % 2
                if isinstance(m, int) and m == 0 and kv == 0:
                    dve.wait_ge(bias_step, 7)
                    nc.vector.tensor_tensor(bias[:, 0], bias[:, 0], bias[:, 1], ALU.max).then_inc(bias_ready, 1)
                    dve.wait_ge(seen_ready, 3)
                elif isinstance(m, int) and m == 1:
                    dve.wait_ge(bias_ready, 1)
                heads = slice(kv * GROUP, (kv + 1) * GROUP)
                carrier.dve_wait(dve, score_full, 2 * m + kv + 1)
                nc.vector.copy_predicated(score[:, heads, P:], earlier_tile.bitcast(mybir.dt.uint32),
                                          score[:, heads, 0:P]).then_inc(take_step, 1)
                carrier.dve_wait(dve, take_step, 2 * m + kv + 1)
                for h in range(kv * GROUP, (kv + 1) * GROUP):
                    last = nc.vector.tensor_tensor_reduce(
                        out=probs[:, b, h], in0=score[:, h, P:], in1=bias[:, 1 if isinstance(m, int) and m == 0 else 0, h],
                        scale=1.0, scalar=sinks[:, h:h + 1], op0=ALU.add, op1=ALU.max, accum_out=rowmax[:, b, h:h + 1])
                last.then_inc(score_taken, 1)
                dve.wait_ge(score_taken, 2 * m + kv + 1)
                nc.vector.tensor_scalar(negmax[:, b, heads], rowmax[:, b, heads], -1.0, None, ALU.mult).then_inc(row_step, 1)
                nc.vector.tensor_tensor(sinkdiff[:, b, heads], sinks[:, heads], rowmax[:, b, heads],
                                        ALU.subtract).then_inc(max_ready, 1)

            def invert(m, b, kv):
                heads = slice(kv * GROUP, (kv + 1) * GROUP)
                dve.wait_ge(exp_done, 2 * m + kv + 1)
                nc.vector.tensor_tensor(denom[:, b, heads], rowsum[:, b, heads], sinkexp[:, b, heads],
                                        ALU.add).then_inc(den_step, 1)
                dve.wait_ge(den_step, 4 * m + 2 * kv + 1)
                nc.vector.reciprocal(inv[:, b, heads], denom[:, b, heads]).then_inc(den_step, 1)

            def pT_copy(m, kv):
                dve.wait_ge(p_turned, 2 * m + kv + 1)
                if isinstance(m, int) and m == 0:
                    dve.wait_ge(seen_ready, 3)
                for tile in range(2):
                    last = nc.vector.tensor_tensor(pT[:, tile, kv, :], turn[kv][:], seen[:, tile], ALU.mult)
                last.then_inc(pT_done, 1)

            def make_k_lo(n):
                p = slot("k")
                if not isinstance(n, int) or n > 0:
                    dve.wait_ge(proj_full, filled(n, p))
                    nc.vector.tensor_copy(k_lo[:, 0:P], k_lo[:, TB:TB + P]).then_inc(k_lo_halo, 1)
                    dve.wait_ge(k_lo_halo, n)
                dve.wait_ge(k_hi_done, n + 1)
                for kv in range(KV):
                    last = nc.vector.tensor_tensor(k_lo[halves[kv], P:], proj[p % 2][halves[kv], :],
                                                   k_hi[halves[kv], kv, P:].bitcast(F32), ALU.subtract)
                last.then_inc(proj_free[p % 2], 1)

            def make_q_lo(n, t):
                p = slot(f"q{t}")
                for odd in range(2):
                    head = 2 * t + odd
                    dve.wait_ge(q_hi_done, HEADS * n + head + 1)
                    kv = head // GROUP
                    last = nc.vector.scalar_tensor_tensor(
                        out=q[halves[1 - kv], head, :], in0=proj[p % 2][halves[odd], :], scalar=HD ** -0.5,
                        in1=q[halves[kv], head, :].bitcast(F32), op0=ALU.mult, op1=ALU.subtract)
                last.then_inc(proj_free[p % 2], 1)

            def gate_make(n, t):
                p = slot(f"g{t}")
                if t == 0:
                    need(dve, gated, n)
                dve.wait_ge(tanh_done, GROUP * n + t + 1)
                nc.vector.scalar_tensor_tensor(out=gate[:, t, :], in0=tanh[:, t % 2, :], scalar=1.0, in1=proj[p % 2][:],
                                               op0=ALU.add, op1=ALU.mult).then_inc(proj_free[p % 2], 1)

            def output(n, j, at):
                dve.wait_ge(proj_full, filled(*at))
                if j == 0:
                    need(dve, y_stored, 16 * n)
                nc.vector.tensor_copy(y[:, :, j * P:(j + 1) * P],
                                      proj[at[1] % 2][:].rearrange("p (t c) -> p t c", t=GROUP)).then_inc(proj_free[at[1] % 2], 1)

            def body(n):
                first, final = isinstance(n, int) and n == 0, isinstance(n, int) and n == NB - 1
                for kk in range(KT):
                    st.split_lo(dve, n, kk)
                    if not first and kk == 1:
                        output(n - 1, 2, (n - 1, slot("o2")))
                    if first and kk == 3:
                        w.split_lo(dve, CHUNK_Q)
                if not first:
                    pT_copy(4 * n - 1, 0)
                    pT_copy(4 * n - 1, 1)
                make_k_lo(n)
                make_q_lo(n, 0)
                if not first:
                    output(n - 1, 3, (n, slot("o3")))
                for t in range(1, GROUP):
                    if first:
                        w.split_lo(dve, CHUNK_Q + t)
                    make_q_lo(n, t)
                    if final and t >= 2:
                        w.split_lo(dve, CHUNK_CB + t - 2)
                for j in range(SUB):
                    for kv in range(KV):
                        take_scores(n, j, kv)
                        if kv == 0 and j:
                            pT_copy(4 * n + j - 1, 0)
                            pT_copy(4 * n + j - 1, 1)
                    invert(4 * n + j, j % 2, 0)
                    if j:
                        gate_make(n, j)
                    invert(4 * n + j, j % 2, 1)
                    if j == 0:
                        gate_make(n, j)
                    if j in (1, 2):
                        output(n, j - 1, (n, slot(f"o{j - 1}")))

            body(0)
            with dve.Fori(1, NB - 1) as n:
                body(n)
            body(NB - 1)
            output(NB - 1, 2, (NB - 1, slot("o2")))
            done, last = slice(0, (SUB - 1) * P), slice((SUB - 1) * P, TB)
            for name in ("g3", "o2"):
                dve.wait_ge(proj_free[slot(name) % 2], earlier(NB - 1, slot(name)) + 1)
            nc.vector.tensor_tensor(y[:, :, done], y[:, :, done], gate[:, :, done], ALU.mult).then_inc(tail_gated, 1)
            pT_copy(4 * NB - 1, 0)
            pT_copy(4 * NB - 1, 1)
            dve.wait_ge(proj_full, filled(NB, 0))
            dve.wait_ge(tail_gated, 1)
            nc.vector.tensor_tensor(y[:, :, last], proj[0][:].rearrange("p (t c) -> p t c", t=GROUP), gate[:, :, last],
                                    ALU.mult).then_inc(gated, 1)

        @block.tensor
        def _(pe):
            def project(n, name, between=None):
                p = slot(name)
                c, half = (CHUNK_K, "kv".index(name)) if name in "kv" else \
                    ((CHUNK_Q if name[0] == "q" else CHUNK_G) + int(name[1]) // 2, int(name[1]) % 2)
                cols = slice(half * P, (half + 1) * P)
                need(pe, proj_free[p % 2], earlier(n, p))
                if isinstance(n, int) and n == 0:
                    pe.wait_ge(w.lo_done[c], 1)
                for kk in range(KT):
                    if name == "k":
                        pe.wait_ge(st.lo_done, st.lo_count(n, kk))
                    last = split3(nc, proj[p % 2][:], w.hi(c)[:, kk, cols], w.lo(c)[:, kk, cols], st.hi[:, kk, :],
                                  st.lo[:, kk, :], kk == 0, kk == KT - 1)
                    if between and kk < KT - 1:
                        between(kk)
                last.then_inc(proj_full, 1)

            def scores(n, j):
                m = 4 * n + j
                keys = slice(j * P, (j + 2) * P)
                for kv in range(KV):
                    need(pe, score_taken, 2 * (m - 1) + kv + 1)
                    rows = halves[kv]
                    for h in range(kv * GROUP, (kv + 1) * GROUP):
                        out, queries = score[:, h, :], q[:, h, j * P:(j + 1) * P]
                        nc.tensor.matmul(out, queries, k_hi[:, kv, keys], start=True, stop=False)
                        last = nc.tensor.matmul(out, queries[rows], k_lo[rows, keys], start=False, stop=True)
                    last.then_inc(score_full, 1)

            def turn_probs(m, j, kv):
                pe.wait_ge(probs_ready, 2 * m + kv + 1)
                for t in range(GROUP):
                    last = nc.tensor.transpose(turn[kv][:, t * P:(t + 1) * P], probs[:, j % 2, kv * GROUP + t], st.ident[:])
                last.then_inc(p_turned, 1)

            def turning(m, j):
                return lambda kk: turn_probs(m, j, kk) if kk < KV else None

            def attend(m, j, at):
                p = at[1]
                need(pe, proj_free[p % 2], earlier(*at))
                pe.wait_ge(pT_done, 2 * m + 2)
                for kv in range(KV):
                    pairs = slice(kv * GROUP // 2 * P, (kv + 1) * GROUP // 2 * P)
                    for kt in range(2):
                        for odd in range(2):
                            weights = pT[:, kt, kv, :].rearrange("p (t o c) -> p t o c", o=2, c=P)[:, :, odd, :]
                            last = nc.tensor.matmul(proj[p % 2][halves[odd], pairs], v[:, j + kt, halves[kv]], weights,
                                                    start=(kt == 0), stop=(kt == 1))
                last.then_inc(proj_full, 1)

            def body(n):
                first = isinstance(n, int) and n == 0
                for kk in range(TURNS):
                    if kk == 2:
                        need(pe, score_taken, 8 * n)
                    st.transpose(pe, n, kk)
                project(n, "k", lambda kk: st.transpose(pe, n, kk + TURNS) if kk + TURNS < KT else None)
                if first:
                    project(n, "q0")
                else:
                    project(n, "q0", turning(4 * n - 1, 3))
                    attend(4 * n - 1, 3, (n, slot("o3")))
                for name in ("q1", "q2", "q3", "v"):
                    project(n, name)
                for name in ("q2", "q3"):
                    pe.wait_ge(proj_free[slot(name) % 2], earlier(n, slot(name)) + 1)

                def turn_v(kk):
                    if kk == 2:
                        pe.wait_ge(proj_free[slot("v") % 2], earlier(n, slot("v")) + 1)
                        for s in range(SUB):
                            last = nc.tensor.transpose(turn[1][:, s * P:(s + 1) * P], vT[:, s * P:(s + 1) * P], st.ident[:])
                        last.then_inc(v_turned, 1)

                for j in range(SUB):
                    scores(n, j)
                    if j == 0:
                        project(n, "g0", turn_v)
                        pe.wait_ge(v_ready, n + 1)
                    else:
                        m = 4 * n + j - 1
                        project(n, f"g{j}", turning(m, j - 1))
                        attend(m, j - 1, (n, slot(f"o{j - 1}")))

            body(0)
            with pe.Fori(1, NB) as n:
                body(n)
            for kv in range(KV):
                turn_probs(4 * NB - 1, 3, kv)
            attend(4 * NB - 1, 3, (NB, 0))


def mixer_phase(nc, st, w, y_out, y_stored, y_conv_stored, y_pool_stored, y_next, y_loaded, y_hi_done, y_lo_done, pool_w, pool_scale, conv_dw,
                conv_b, conv_ln_g, conv_ln_b, conv_pw, y_scratch):
    ctx = ExitStack()
    with ctx:
        sb = lambda name, shape, dt=F32: ctx.enter_context(nc.sbuf_tensor("m_" + name, shape, dt))
        sem = lambda name: ctx.enter_context(nc.semaphore("m_" + name))
        pool_carrier = Carrier(nc, ctx, "m_pool_carrier")
        dve_carrier = Carrier(nc, ctx, "m_dve_carrier")
        bank = lambda name, shape: ctx.enter_context(nc.psum_tensor("m_" + name, shape, F32))
        proj = [bank(f"proj{b}", [P, TB]) for b in range(2)]
        tok = [bank(f"tok{b}", [P, 2, CONV_W]) for b in range(2)]
        feat = [bank(f"feat{b}", [P, TB]) for b in range(2)]
        st.use(NB, [bank(f"turn{b}", [P, TB]) for b in range(2)] + feat, sb("squares", [P, D]))
        w.use({CHUNK_U: y_next[:, 0:4], CHUNK_GP: y_next[:, 4:8], CHUNK_GC: y_next[:, 0:4], CHUNK_OUT: y_next,
               CHUNK_OUT + 1: st.xs})
        CHUNK_OF = {"cb": CHUNK_CB, "ca": CHUNK_CA, "u": CHUNK_U, "gp": CHUNK_GP, "gc": CHUNK_GC}

        sig = sb("sig", [P, 2, TB])
        h = sb("h", [P, 2, PAD + TB])
        conv = sb("conv", [P, 2, TB])
        taps = sb("taps", [P, 2, TAPS])
        conv_bias = sb("conv_bias", [P, 2])
        ln_gain = sb("ln_gain", [P, 2])
        ln_bias = sb("ln_bias", [P, 2])
        stats = sb("stats", [P, SUB, 6])
        meanvar = sb("meanvar", [P, SUB, 2])
        var_eps = sb("var_eps", [P, SUB])
        ln_rstd = sb("ln_rstd", [P, SUB])
        neg_mean = sb("neg_mean", [P, SUB])
        ln_shift = sb("ln_shift", [P, SUB])
        z = sb("z", [P, SUB, CONV_W])
        hs = sb("hs", [P, 2, TB])
        pw = sb("pw", [P, 2, CONV_W])
        u = sb("u", [P, 2, HALO + TB])
        sums = sb("sums", [P, 2, 2, HALO + TB])
        diff = sb("diff", [P, 2, TB])
        count = sb("count", [P, 2, HALO])
        widen = sb("widen", [P, 2, HALO])
        pool_lhs = sb("pool_lhs", [P, 2, P])
        pscale = sb("pscale", [P, 2, P])
        pool_map = sb("pool_map", [P, 2, P])
        gate_p = sb("gate_p", [P, 2, TB])
        gate_c = sb("gate_c", [P, 2, TB])
        y_pool, y_conv = y_out[:, 0:2], y_out[:, 2:4]

        small_loaded = sem("small_loaded")
        pool_w_zero = sem("pool_w_zero")
        halo_zero = sem("halo_zero")
        taps_ready = sem("taps_ready")
        pool_lhs_ready = sem("pool_lhs_ready")
        count_step = sem("count_step")
        widen_ready = sem("widen_ready")
        sums_done = sem("sums_done")
        means_done = sem("means_done")
        proj_full = sem("proj_full")
        proj_free = [sem("proj_free0"), sem("proj_free1")]
        h_halo = [sem("h_halo0"), sem("h_halo1")]
        tap_done = [sem("tap_done0"), sem("tap_done1")]
        conv_turned = sem("conv_turned")
        stats_done = sem("stats_done")
        meanvar_done = sem("meanvar_done")
        rstd_step = sem("rstd_step")
        z_done = sem("z_done")
        z_turned = sem("z_turned")
        hs_done = sem("hs_done")
        u_halo = sem("u_halo")
        pool_step = sem("pool_step")
        diff_done = sem("diff_done")
        y_pool_done = sem("y_pool_done")
        y_conv_done = sem("y_conv_done")

        SLOT = {name: p for p, name in enumerate(
            ["cb0", "ca0", "cb1", "ca1", "u0", "u1", "pw0", "pw1", "gp0", "gp1", "gc0", "gc1", "po0", "po1"])}
        USES = len(SLOT)

        def early(n, p):
            return isinstance(n, int) and n == 0 and p < SLOT["pw0"]

        def filled(n, p):
            return USES * n + p + 1 - (0 if early(n, p) else 2)

        def earlier(n, p):
            return USES // 2 * n + p // 2 - (0 if early(n, p) else 1)

        block = ctx.enter_context(nc.Block())

        @block.sync
        def _(sp):
            w.load(sp, CHUNK_U)
            w.load(sp, CHUNK_GP)
            with nc.allow_non_contiguous_dma(reason="per-channel constants, once"):
                for i in range(2):
                    cols = slice(i * P, (i + 1) * P)
                    sp.dma_start(taps[:, i, :], conv_dw[0, :, cols].rearrange("j p -> p j")).then_inc(small_loaded, 16)
                    for dst, src in ((conv_bias, conv_b), (ln_gain, conv_ln_g), (ln_bias, conv_ln_b)):
                        sp.dma_start(dst[:, i:i + 1], src[0, cols].rearrange("(p a) -> p a", a=1)).then_inc(small_loaded, 16)
            sp.dma_start(pw[:], conv_pw[0].rearrange("(i p) d -> p i d", p=P)).then_inc(small_loaded, 16)
            sp.dma_start(pscale.rearrange("p i d -> p (i d)"), pool_scale[0:1, :].to_broadcast([P, 2 * P])).then_inc(small_loaded, 16)
            sp.wait_ge(pool_w_zero, 1)
            for g in range(4):
                half = slice(g % 2 * 64, g % 2 * 64 + 64)
                sp.dma_start(pool_map[half, g // 2, half], pool_w[0, g]).then_inc(small_loaded, 16)

            def store_pool(n):
                sp.wait_ge(y_pool_done, 2 * n + 2)
                sp.dma_start(y_scratch[Y_POOL:Y_POOL + 2, :, bass.ds(n * TB, TB)].rearrange("t p c -> p t c"),
                             y_pool[:]).then_inc(y_pool_stored, 16)

            def store_conv(n):
                sp.wait_ge(y_conv_done, 2 * n + 2)
                sp.dma_start(y_scratch[Y_CONV:Y_CONV + 2, :, bass.ds(n * TB, TB)].rearrange("t p c -> p t c"),
                             y_conv[:]).then_inc(y_conv_stored, 16)

            st.load(sp, 1)
            sp.wait_ge(w.lo_done[CHUNK_U], 1)
            w.load(sp, CHUNK_GC)
            store_pool(0)
            with sp.Fori(1, NB - 1) as n:
                st.load(sp, n + 1)
                store_conv(n - 1)
                store_pool(n)
            w.load(sp, CHUNK_OUT)
            sp.wait_ge(st.turned, KT * 2 * NB)
            w.load(sp, CHUNK_OUT + 1)
            store_conv(NB - 2)
            for stored, count in ((y_stored, 16 * NB), (y_pool_stored, 16), (y_conv_stored, 16)):
                sp.wait_ge(stored, count)
            sp.wait_ge(w.lo_done[CHUNK_OUT], 1)
            sp.dma_start(y_next[:], y_scratch[:, :, 0:TB].rearrange("t p c -> p t c")).then_inc(y_loaded, 16)
            store_pool(NB - 1)
            store_conv(NB - 1)

        SMALL = 16 * (2 * 4 + 1 + 1 + 4)

        @block.gpsimd
        def _(pool):
            carrier = pool_carrier
            carrier.prepare(pool)
            nc.gpsimd.memset(pool_map[:], 0.0).then_inc(pool_w_zero, 1)
            for i in range(2):
                nc.gpsimd.iota(count[:, i, :], pattern=[[1, HALO]], base=1, channel_multiplier=0,
                               allow_small_or_imprecise_dtypes=True).then_inc(count_step, 1)
            pool.wait_ge(count_step, 2)

            def window_sums(n):
                pool.wait_ge(proj_free[0], earlier(n, SLOT["u0"]) + 1)
                pool.wait_ge(proj_free[1], earlier(n, SLOT["u1"]) + 1)
                step = 4 * n
                for i in range(2):
                    cur, width = u[:, i, :], 1
                    for level in range(2 * (i + 1)):
                        dst = sums[:, i, level % 2, :]
                        add = nc.gpsimd.tensor_tensor(dst[:, 2 * width:], cur[:, 2 * width:], cur[:, width:HALO + TB - width],
                                                      ALU.add)
                        cur, width = dst, 2 * width
                        if level < 2 * i + 1:
                            add.then_inc(pool_step, 1)
                            step += 1
                            pool.wait_ge(pool_step, step)
                    add.then_inc(sums_done, 1)

            def window_diffs(n):
                for i in range(2):
                    pool.wait_ge(means_done, 2 * n + i + 1)
                    if isinstance(n, int) and n == 0:
                        nc.gpsimd.tensor_tensor(diff[:, i, 0:HALO], diff[:, i, 0:HALO], widen[:, i, :],
                                                ALU.mult).then_inc(widen_ready, 1)
                        pool.wait_ge(widen_ready, 2 + i)
                    nc.gpsimd.tensor_tensor(diff[:, i, :], diff[:, i, :], u[:, i, HALO:], ALU.subtract).then_inc(diff_done, 1)

            def layer_norm_rstd(n):
                carrier.pool_wait(pool, meanvar_done, SUB * n + SUB)
                nc.gpsimd.tensor_scalar(var_eps[:], meanvar[:, :, 1], EPS, 1.0, ALU.add, ALU.mult).then_inc(rstd_step, 1)
                nc.gpsimd.tensor_scalar(neg_mean[:], meanvar[:, :, 0], -1.0, 1.0, ALU.mult, ALU.mult).then_inc(rstd_step, 1)
                pool.wait_ge(rstd_step, 4 * n + 2)
                nc.gpsimd.tensor_tensor(ln_rstd[:], var_eps[:], st.neg_half[:], ALU.pow).then_inc(rstd_step, 1)
                pool.wait_ge(rstd_step, 4 * n + 3)
                nc.gpsimd.tensor_tensor(ln_shift[:], neg_mean[:], ln_rstd[:], ALU.mult).then_inc(rstd_step, 1)

            def gate_conv(n, at):
                for i in range(2):
                    pool.wait_ge(proj_free[i], earlier(at[0], at[1] + i) + 1)
                    nc.gpsimd.tensor_tensor(y_conv[:, i, :], y_conv[:, i, :], gate_c[:, i, :], ALU.mult).then_inc(y_conv_done, 1)

            def gate_pool(n):
                for i in range(2):
                    pool.wait_ge(proj_free[i], earlier(n, SLOT[f"po{i}"]) + 1)
                    nc.gpsimd.tensor_tensor(y_pool[:, i, :], y_pool[:, i, :], gate_p[:, i, :], ALU.mult).then_inc(y_pool_done, 1)

            def body(n, more):
                if isinstance(n, int) and n == 0:
                    for c in (CHUNK_U, CHUNK_GP):
                        w.split_lo_on_pool(pool, c)
                    pool.wait_ge(widen_ready, 1)
                else:
                    layer_norm_rstd(n - 1)
                if more:
                    st.scale(pool, n + 1, carrier)
                if isinstance(n, int) and n == 0:
                    w.split_lo_on_pool(pool, CHUNK_GC)
                window_sums(n)
                if not isinstance(n, int) or n > 0:
                    gate_conv(n - 1, (n, SLOT["pw0"]))
                window_diffs(n)
                if isinstance(n, int) and n == NB - 1:
                    w.split_lo_on_pool(pool, CHUNK_OUT)
                if isinstance(n, int) and n == NB - 1:
                    layer_norm_rstd(n)
                gate_pool(n)

            body(0, True)
            with pool.Fori(1, NB - 1) as n:
                body(n, True)
            body(NB - 1, False)

        @block.scalar
        def _(act):
            def from_proj(n, name, out, func, scale=1.0):
                p = SLOT[name]
                act.wait_ge(proj_full, filled(n, p))
                nc.scalar.activation(out, proj[p % 2][:], func, scale=scale).then_inc(proj_free[p % 2], 1)

            def layer_norm_apply(n):
                act.wait_ge(rstd_step, 4 * n + 4)
                for s in range(SUB):
                    nc.scalar.activation(z[:, s, :], tok[s // 2][:, s % 2, :], ACT.Identity, scale=ln_rstd[:, s:s + 1],
                                         bias=ln_shift[:, s:s + 1]).then_inc(z_done, 1)

            def norm_silu(n):
                for i in range(2):
                    act.wait_ge(z_turned, 2 * n + i + 1)
                    nc.scalar.activation(hs[:, i, :], feat[i][:], ACT.Silu, scale=ln_gain[:, i:i + 1],
                                         bias=ln_bias[:, i:i + 1]).then_inc(hs_done, 1)

            def copy_conv(n, at):
                need(act, y_conv_stored, 16 * n)
                for i in range(2):
                    p = at[1] + i
                    act.wait_ge(proj_full, filled(at[0], p))
                    nc.scalar.activation(y_conv[:, i, :], proj[p % 2][:], ACT.Copy).then_inc(proj_free[p % 2], 1)

            def window_means(n):
                for i in range(2):
                    act.wait_ge(sums_done, 2 * n + i + 1)
                    for g in (2 * i, 2 * i + 1):
                        half = slice(g % 2 * 64, g % 2 * 64 + 64)
                        last = nc.scalar.activation(diff[half, i, :], sums[half, i, g % 2, HALO:], ACT.Copy,
                                                    scale=1.0 / POOL_WINDOWS[g])
                    last.then_inc(means_done, 1)

            def body(n, more):
                first, final = isinstance(n, int) and n == 0, isinstance(n, int) and n == NB - 1
                for kk in range(KT):
                    st.split_hi(act, n, kk)
                from_proj(n, "cb0", sig[:, 0, :], ACT.Tanh, 0.5)
                if first:
                    w.split_hi(act, CHUNK_U)
                if not first:
                    layer_norm_apply(n - 1)
                from_proj(n, "cb1", sig[:, 1, :], ACT.Tanh, 0.5)
                if first:
                    w.split_hi(act, CHUNK_GP)
                if more:
                    st.square(act, n + 1)
                if first:
                    w.split_hi(act, CHUNK_GC)
                if not first:
                    norm_silu(n - 1)
                act.wait_ge(proj_full, filled(n, SLOT["u0"]))
                if first:
                    act.wait_ge(halo_zero, 2)
                else:
                    act.wait_ge(diff_done, 2 * n)
                    nc.scalar.activation(u[:, :, 0:HALO], u[:, :, TB:], ACT.Copy).then_inc(u_halo, 1)
                    act.wait_ge(u_halo, n)
                for i in range(2):
                    from_proj(n, f"u{i}", u[:, i, HALO:], ACT.Copy)
                if not first:
                    copy_conv(n - 1, (n, SLOT["pw0"]))
                    act.wait_ge(y_pool_done, 2 * n)
                if final:
                    w.split_hi(act, CHUNK_OUT)
                from_proj(n, "gp0", gate_p[:, 0, :], ACT.Silu)
                window_means(n)
                from_proj(n, "gp1", gate_p[:, 1, :], ACT.Silu)
                if final:
                    w.split_hi(act, CHUNK_OUT + 1)
                if not first:
                    act.wait_ge(y_conv_done, 2 * n)
                for i in range(2):
                    from_proj(n, f"gc{i}", gate_c[:, i, :], ACT.Silu)
                if first:
                    act.wait_ge(y_stored, 16 * NB)
                    act.wait_ge(small_loaded, SMALL)
                else:
                    act.wait_ge(y_pool_stored, 16 * n)
                for i in range(2):
                    p = SLOT[f"po{i}"]
                    act.wait_ge(proj_full, filled(n, p))
                    nc.scalar.activation(y_pool[:, i, :], proj[p % 2][:], ACT.Copy).then_inc(proj_free[p % 2], 1)

            body(0, True)
            with act.Fori(1, NB - 1) as n:
                body(n, True)
            body(NB - 1, False)
            def split_y(first, end):
                for kk in range(first, end):
                    nc.scalar.activation(st.hi[:, kk, :], y_next[:, kk, :], ACT.Copy).then_inc(y_hi_done, 1)

            layer_norm_apply(NB - 1)
            act.wait_ge(y_loaded, 16)
            split_y(0, 3)
            norm_silu(NB - 1)
            split_y(3, KT)

        @block.vector
        def _(dve):
            carrier = dve_carrier
            carrier.prepare(dve)
            nc.vector.memset(h[:, :, 0:PAD], 0.0).then_inc(halo_zero, 1)
            nc.vector.memset(u[:, :, 0:HALO], 0.0).then_inc(halo_zero, 1)
            dve.wait_ge(halo_zero, 2)

            def prepare_constants():
                dve.wait_ge(small_loaded, SMALL)
                nc.vector.tensor_scalar(taps[:], taps[:], 0.5, None, ALU.mult).then_inc(taps_ready, 1)
                nc.vector.tensor_tensor(pool_lhs[:], pool_map[:], pscale[:], ALU.mult).then_inc(pool_lhs_ready, 1)
                dve.wait_ge(count_step, 2)
                for g, window in enumerate(POOL_WINDOWS):
                    half = slice(g % 2 * 64, g % 2 * 64 + 64)
                    nc.vector.tensor_scalar(count[half, g // 2, :], count[half, g // 2, :], 1.0 / window, 1.0, ALU.mult,
                                            ALU.min).then_inc(count_step, 1)
                dve.wait_ge(count_step, 6)
                nc.vector.reciprocal(widen[:], count[:]).then_inc(widen_ready, 1)
                dve.wait_ge(taps_ready, 1)

            def glu(n, i):
                p = SLOT[f"ca{i}"]
                if not (isinstance(n, int) and n == 0):
                    dve.wait_ge(tap_done[i], TAPS * n)
                    nc.vector.tensor_copy(h[:, i, 0:PAD], h[:, i, TB:]).then_inc(h_halo[i], 1)
                    dve.wait_ge(h_halo[i], n)
                b = SLOT[f"cb{i}"]
                dve.wait_ge(proj_free[b % 2], earlier(n, b) + 1)
                dve.wait_ge(proj_full, filled(n, p))
                nc.vector.scalar_tensor_tensor(out=h[:, i, PAD:], in0=sig[:, i, :], scalar=1.0, in1=proj[p % 2][:],
                                               op0=ALU.add, op1=ALU.mult).then_inc(proj_free[p % 2], 1)

            def tap(n, i, j):
                if j == 0:
                    p = SLOT[f"ca{i}"]
                    dve.wait_ge(proj_free[p % 2], earlier(n, p) + 1)
                    need(dve, conv_turned, 2 * n)
                    nc.vector.tensor_scalar(conv[:, i, :], h[:, i, 0:TB], taps[:, i, 0:1], conv_bias[:, i:i + 1],
                                            ALU.mult, ALU.add).then_inc(tap_done[i], 1)
                else:
                    dve.wait_ge(tap_done[i], TAPS * n + j)
                    nc.vector.scalar_tensor_tensor(out=conv[:, i, :], in0=h[:, i, j:j + TB], scalar=taps[:, i, j:j + 1],
                                                   in1=conv[:, i, :], op0=ALU.mult, op1=ALU.add).then_inc(tap_done[i], 1)

            def layer_norm_stats(n):
                for s in range(SUB):
                    dve.wait_ge(conv_turned, 2 * n + s // 2 + 1)
                    nc.vector.bn_stats(stats[:, s, :], tok[s // 2][:, s % 2, :]).then_inc(stats_done, 1)
                carrier.dve_wait(dve, stats_done, SUB * n + SUB)
                for s in range(SUB):
                    nc.vector.bn_aggr(meanvar[:, s, :], stats[:, s, :]).then_inc(meanvar_done, 1)

            LEAD = 12
            ORDER = [(0, j) for j in range(LEAD)]
            for j in range(LEAD, TAPS):
                ORDER += [(0, j), (1, j - LEAD)]
            ORDER += [(1, j) for j in range(TAPS - LEAD, TAPS)]

            def some_taps(n, lo, hi):
                for i, j in ORDER[lo:hi]:
                    tap(n, i, j)

            def body(n):
                first = isinstance(n, int) and n == 0
                for kk in range(KT):
                    st.split_lo(dve, n, kk)
                if not first:
                    layer_norm_stats(n - 1)
                glu(n, 0)
                if first:
                    prepare_constants()
                some_taps(n, 0, LEAD)
                glu(n, 1)
                some_taps(n, LEAD, len(ORDER))

            body(0)
            with dve.Fori(1, NB) as n:
                body(n)
            layer_norm_stats(NB - 1)
            for kk in range(KT):
                dve.wait_ge(y_hi_done, kk + 1)
                nc.vector.tensor_tensor(st.lo[:, kk, :], y_next[:, kk, :], st.hi[:, kk, :].bitcast(F32),
                                        ALU.subtract).then_inc(y_lo_done, 1)
            dve.wait_ge(y_conv_stored, 16 * (NB - 1))
            for i in range(2):
                dve.wait_ge(proj_full, filled(NB, i))
                nc.vector.tensor_tensor(y_conv[:, i, :], proj[i][:], gate_c[:, i, :], ALU.mult).then_inc(y_conv_done, 1)

        @block.tensor
        def _(pe):
            def project(n, name, between=None):
                p, c = SLOT[name], CHUNK_OF[name[:-1]]
                cols = slice(int(name[-1]) * P, int(name[-1]) * P + P)
                need(pe, proj_free[p % 2], earlier(n, p))
                if isinstance(n, int) and n == 0:
                    pe.wait_ge(w.lo_done[c], 1)
                for kk in range(KT):
                    if name == "cb0":
                        pe.wait_ge(st.lo_done, st.lo_count(n, kk))
                    last = split3(nc, proj[p % 2][:], w.hi(c)[:, kk, cols], w.lo(c)[:, kk, cols], st.hi[:, kk, :],
                                  st.lo[:, kk, :], kk == 0, kk == KT - 1)
                    if between:
                        between(kk)
                last.then_inc(proj_full, 1)

            def turn_conv(n):
                for i in range(2):
                    pe.wait_ge(tap_done[i], TAPS * n + TAPS)
                for b in range(2):
                    for s in (2 * b, 2 * b + 1):
                        for i in range(2):
                            last = nc.tensor.transpose(tok[b][:, s % 2, i * P:(i + 1) * P],
                                                       conv[:, i, s * P:(s + 1) * P], st.ident[:])
                    last.then_inc(conv_turned, 1)

            def turn_z(n):
                pe.wait_ge(z_done, SUB * n + SUB)
                for i in range(2):
                    for s in range(SUB):
                        last = nc.tensor.transpose(feat[i][:, s * P:(s + 1) * P], z[:, s, i * P:(i + 1) * P], st.ident[:])
                    last.then_inc(z_turned, 1)

            def pointwise(n, at):
                pe.wait_ge(hs_done, 2 * n + 2)
                for o in range(2):
                    p = at[1] + o
                    need(pe, proj_free[p % 2], earlier(at[0], p))
                    for i in range(2):
                        last = nc.tensor.matmul(proj[p % 2][:], pw[:, i, o * P:(o + 1) * P], hs[:, i, :],
                                                start=(i == 0), stop=(i == 1))
                    last.then_inc(proj_full, 1)

            def map_pool(n):
                pe.wait_ge(diff_done, 2 * n + 2)
                if isinstance(n, int) and n == 0:
                    pe.wait_ge(pool_lhs_ready, 1)
                for i in range(2):
                    p = SLOT[f"po{i}"]
                    need(pe, proj_free[p % 2], earlier(n, p))
                    nc.tensor.matmul(proj[p % 2][:], pool_lhs[:, i, :], diff[:, i, :], start=True, stop=True).then_inc(proj_full, 1)

            def body(n):
                first = isinstance(n, int) and n == 0
                for kk in range(TURNS):
                    st.transpose(pe, n, kk)
                if not first:
                    turn_conv(n - 1)
                project(n, "cb0", lambda kk: st.transpose(pe, n, kk + TURNS) if kk + TURNS < KT else None)
                project(n, "ca0")
                project(n, "cb1")
                project(n, "ca1")
                if not first:
                    turn_z(n - 1)
                project(n, "u0")
                project(n, "u1")
                if first:
                    pe.wait_ge(small_loaded, SMALL)
                else:
                    pointwise(n - 1, (n, SLOT["pw0"]))
                for name in ("gp0", "gp1", "gc0", "gc1"):
                    project(n, name)
                if isinstance(n, int) and n == NB - 1:
                    turn_conv(n)
                map_pool(n)

            body(0)
            with pe.Fori(1, NB - 1) as n:
                body(n)
            body(NB - 1)
            turn_z(NB - 1)
            pointwise(NB - 1, (NB, 0))


def output_phase(nc, st, w, y_out, y, y_loaded, y_hi_done, y_lo_done, y_conv_stored, y_pool_stored, x, final_g, y_scratch, out):
    ctx = ExitStack()
    with ctx:
        sb = lambda name, shape, dt=F32: ctx.enter_context(nc.sbuf_tensor("o_" + name, shape, dt))
        sem = lambda name: ctx.enter_context(nc.semaphore("o_" + name))
        pool_carrier = Carrier(nc, ctx, "o_pool_carrier")
        y_hi = [st.hi, sb("y_hi", [P, KT, TB], F32R)]
        y_lo = [st.lo, sb("y_lo", [P, KT, TB], F32R)]
        xs = [st.xs, sb("xs", [P, SUB, D])]
        squares = w.hi_buf[:, SLOTS - 1, 0:D]
        gain = sb("gain", [P, D])
        res = y_out.rearrange("p (b t) c -> p b (t c)", b=2)
        sumsq = sb("sumsq", [P, 2, SUB])
        meansq = sb("meansq", [P, 2, SUB])
        rstd = sb("rstd", [P, 2, SUB])
        neg_half = sb("neg_half", [P, 1])
        acc = [ctx.enter_context(nc.psum_tensor(f"o_acc{b}", [P, TB], F32)) for b in range(4)]

        gain_loaded = sem("gain_loaded")
        half_ready = sem("half_ready")
        x_loaded = [sem("x_loaded0"), sem("x_loaded1")]
        acc_full = sem("acc_full")
        added = sem("added")
        squared = sem("squared")
        rstd_step = sem("rstd_step")
        finished = sem("finished")
        stored = [sem("stored0"), sem("stored1")]

        block = ctx.enter_context(nc.Block())

        @block.sync
        def _(sp):
            def load_x(n, b):
                need(sp, finished, SUB * (n - 1))
                sp.dma_start(xs[b][:], x[0, bass.ds(n * TB, TB), :].rearrange("(s p) d -> p s d", p=P)).then_inc(x_loaded[b], 16)

            def store(n, s):
                sp.wait_ge(finished, SUB * n + s + 1)
                sp.dma_start(out[0, bass.ds(n * TB + s * P, P), :], res[:, s % 2, :]).then_inc(stored[s % 2], 16)

            sp.dma_start(gain[:], final_g.rearrange("(a d) -> a d", a=1).to_broadcast([P, D])).then_inc(gain_loaded, 16)
            sp.wait_ge(w.lo_done[CHUNK_OUT + 1], 1)
            st.load(sp, NB, 0)
            load_x(1, 1)

            def body(n, b, more):
                for s in range(SUB):
                    store(n, s)
                if more:
                    load_x(n + 2, b)

            with sp.Fori(0, NB // 2 - 1) as pair:
                body(2 * pair, 0, True)
                body(2 * pair + 1, 1, True)
            body(NB - 2, 0, False)
            body(NB - 1, 1, False)
            for b in range(2):
                sp.wait_ge(stored[b], 16 * 2 * NB)
            sp.wait_ge(y_pool_stored, 16 * NB)
            sp.wait_ge(y_conv_stored, 16 * NB)

        @block.gpsimd
        def _(pool):
            carrier = pool_carrier
            carrier.prepare(pool)
            nc.gpsimd.memset(neg_half[:], -0.5).then_inc(half_ready, 1)
            pool.wait_ge(half_ready, 1)

            def body(n, b):
                for s in range(SUB):
                    col = slice(s, s + 1)
                    carrier.pool_wait(pool, squared, SUB * n + s + 1)
                    nc.gpsimd.tensor_scalar(meansq[:, b, col], sumsq[:, b, col], 1.0 / D, EPS, ALU.mult,
                                            ALU.add).then_inc(rstd_step, 1)
                    pool.wait_ge(rstd_step, 2 * SUB * n + 2 * s + 1)
                    nc.gpsimd.tensor_tensor(rstd[:, b, col], meansq[:, b, col], neg_half[:], ALU.pow).then_inc(rstd_step, 1)

            with pool.Fori(0, NB, 2) as n:
                body(n, 0)
                body(n + 1, 1)

        @block.scalar
        def _(act):
            def load_y(n):
                need(act, y_lo_done, KT * n)
                act.dma_start(y[:], y_scratch[:, :, bass.ds(n * TB, TB)].rearrange("t p c -> p t c")).then_inc(y_loaded, 16)

            def split(n, b, k):
                act.wait_ge(y_loaded, 16 * n + 16)
                if k == 0:
                    need(act, acc_full, 8 * n - 8)
                nc.scalar.activation(y_hi[b][:, k, :], y[:, k, :], ACT.Copy).then_inc(y_hi_done, 1)

            def body(n, b, more):
                for s in range(SUB):
                    if more:
                        split(n + 1, 1 - b, 2 * s)
                        split(n + 1, 1 - b, 2 * s + 1)
                    act.wait_ge(added, 8 * n + 2 * s + 2)
                    if not isinstance(n, int) or n > 0 or s > 0:
                        act.wait_ge(squared, SUB * n + s)
                    nc.scalar.activation(squares, xs[b][:, s, :], ACT.Square,
                                         accum_out=sumsq[:, b, s:s + 1]).then_inc(squared, 1)
                if more > 1:
                    if isinstance(n, int) and n == NB - 3:
                        act.wait_ge(y_pool_stored, 16 * NB)
                        act.wait_ge(y_conv_stored, 16 * NB)
                    load_y(n + 2)

            load_y(1)
            body(0, 0, NB - 1)
            with act.Fori(1, NB - 3, 2) as n:
                body(n, 1, 2)
                body(n + 1, 0, 2)
            body(NB - 3, 1, 2)
            body(NB - 2, 0, 1)
            body(NB - 1, 1, 0)

        @block.vector
        def _(dve):
            def split(n, b, k):
                dve.wait_ge(y_hi_done, KT * n + k + 1)
                nc.vector.tensor_tensor(y_lo[b][:, k, :], y[:, k, :], y_hi[b][:, k, :].bitcast(F32),
                                        ALU.subtract).then_inc(y_lo_done, 1)

            w.split_lo(dve, CHUNK_OUT + 1)
            dve.wait_ge(gain_loaded, 16)
            dve.wait_ge(y_pool_stored, 16 * NB)
            dve.wait_ge(y_conv_stored, 16 * NB)

            def finish(n, b, s):
                dve.wait_ge(rstd_step, 2 * SUB * n + 2 * s + 2)
                if not isinstance(n, int) or n > 0 or s >= 2:
                    dve.wait_ge(stored[s % 2], 16 * 2 * n + 16 * (s // 2))
                nc.vector.scalar_tensor_tensor(out=res[:, s % 2, :], in0=xs[b][:, s, :], scalar=rstd[:, b, s:s + 1],
                                               in1=gain[:], op0=ALU.mult, op1=ALU.mult).then_inc(finished, 1)

            def body(n, b, more, uses):
                if uses is not None:
                    dve.wait_ge(x_loaded[b], uses)
                for s in range(SUB):
                    if uses is None:
                        dve.wait_ge(st.loaded[s], 16 * (2 * NB + 1))
                    if more:
                        split(n + 1, 1 - b, 2 * s)
                        split(n + 1, 1 - b, 2 * s + 1)
                    for half in range(2):
                        cols = slice(half * TB, (half + 1) * TB)
                        dve.wait_ge(acc_full, 8 * n + 2 * s + half + 1)
                        nc.vector.tensor_tensor(xs[b][:, s, cols], acc[s % 2 * 2 + half][:], xs[b][:, s, cols],
                                                ALU.add).then_inc(added, 1)
                    if s:
                        finish(n, b, s - 1)
                finish(n, b, SUB - 1)

            body(0, 0, True, None)
            with dve.Fori(1, NB - 1, 2) as n:
                body(n, 1, True, 8 * n + 8)
                body(n + 1, 0, True, 8 * n + 8)
            body(NB - 1, 1, False, 8 * NB)

        @block.tensor
        def _(pe):
            def body(n, b):
                for s in range(SUB):
                    toks = slice(s * P, (s + 1) * P)
                    for half in range(2):
                        w_hi, w_lo = w.hi(CHUNK_OUT + half), w.lo(CHUNK_OUT + half)
                        if isinstance(n, int) and n == 0 and s == 0:
                            pe.wait_ge(w.lo_done[CHUNK_OUT + half], 1)
                        bank = s % 2 * 2 + half
                        if not isinstance(n, int) or n > 0 or s >= 2:
                            pe.wait_ge(added, 8 * n + 2 * s + half - 3)
                        for k in range(KT):
                            if s == 0 and half == 0:
                                pe.wait_ge(y_lo_done, KT * n + k + 1)
                            last = split3(nc, acc[bank][:], y_hi[b][:, k, toks], y_lo[b][:, k, toks],
                                          w_hi[:, k, :], w_lo[:, k, :], k == 0, k == KT - 1)
                        last.then_inc(acc_full, 1)

            body(0, 0)
            with pe.Fori(1, NB - 1, 2) as n:
                body(n, 1)
                body(n + 1, 0)
            body(NB - 1, 1)


def build(nc, x, ln_g, w_in, pool_w, pool_scale, conv_dw, conv_b, conv_ln_g, conv_ln_b, conv_pw, attn_sinks,
          w_out, final_g, out):
    y_scratch = nc.dram_tensor("y_scratch", (KT, P, S), F32, kind="Internal").ap()
    ctx = ExitStack()
    with ctx:
        sem = lambda name: ctx.enter_context(nc.semaphore(name))
        st = XStage(nc, ctx, x, ln_g)
        w = Weights(nc, ctx, w_in, w_out)
        y_out = ctx.enter_context(nc.sbuf_tensor("y_out", [P, 4, TB], F32))
        y_attn_stored, y_pool_stored, y_conv_stored = sem("y_attn_stored"), sem("y_pool_stored"), sem("y_conv_stored")
        attention_phase(nc, st, w, y_out, y_attn_stored, attn_sinks, y_scratch)
        y_loaded = sem("y_loaded")
        y_hi_done, y_lo_done = sem("y_hi_done"), sem("y_lo_done")
        y = ctx.enter_context(nc.sbuf_tensor("y", [P, KT, TB], F32))
        mixer_phase(nc, st, w, y_out, y_attn_stored, y_conv_stored, y_pool_stored, y, y_loaded, y_hi_done, y_lo_done, pool_w, pool_scale,
                    conv_dw, conv_b, conv_ln_g, conv_ln_b, conv_pw, y_scratch)
        output_phase(nc, st, w, y_out, y, y_loaded, y_hi_done, y_lo_done, y_conv_stored, y_pool_stored, x, final_g, y_scratch, out)


_INS = ["x", "ln_g", "w_in", "pool_w", "pool_scale", "conv_dw", "conv_b", "conv_ln_g", "conv_ln_b", "conv_pw",
        "attn_sinks", "w_out", "final_g"]


def kernel(**inputs):
    import numpy as _np
    import concourse.bacc as _bacc
    from concourse import mybir as _mybir
    from concourse.bass_utils import run_bass_kernel_spmd as _run

    nc = _bacc.Bacc("TRN2", target_bir_lowering=False, num_devices=1)
    arrays, args = {}, []
    for name in _INS:
        a = _np.ascontiguousarray(inputs[name])
        arrays[f"in_{name}_dram"] = a
        args.append(nc.dram_tensor(f"in_{name}_dram", a.shape, _mybir.dt.from_np(a.dtype), kind="ExternalInput").ap())
    out = nc.dram_tensor("out_dram", (1, S, D), _mybir.dt.float32, kind="ExternalOutput").ap()
    build(nc, *args, out)
    r = _run(nc, [arrays], core_ids=[0])
    return r.results[0]["out_dram"]
```
